# Optimizing a Trainium2 kernel written in Bass

```python
import math
import jax, jax.numpy as jnp
from jax import lax
import numpy as np

D_MODEL = 1024
BATCH = 1
SEQ = 256
DEPTH = 2

ROPE_THETA = 500000.0
NORM_EPS = 1e-6
QBLOCK = 128
N_BRANCH = 3

MLA_HEADS = 8
MLA_NOPE = 64
MLA_ROPE = 32
MLA_V = 64
MLA_Q_RANK = 384
MLA_KV_RANK = 256

HEAD_DIM = 64
PARTIAL_ROT_DIM = HEAD_DIM // 4

DIL_CONFIGS = ((128, 1), (512, 4), (2048, 16))
DIL_GROUPS = len(DIL_CONFIGS)
DIL_HEADS = 6

DIFF_HEADS = 4

D_FF = 2816
CONV_WIDTH = 3

GATE_COLS = N_BRANCH * D_MODEL
MLA_COLS = MLA_Q_RANK + MLA_KV_RANK + MLA_ROPE
DIL_COLS = DIL_GROUPS * 3 * DIL_HEADS * HEAD_DIM
DIFF_COLS = 3 * DIFF_HEADS * 2 * HEAD_DIM
IN_COLS = GATE_COLS + MLA_COLS + DIL_COLS + DIFF_COLS
SPLITS = [GATE_COLS, GATE_COLS + MLA_COLS, GATE_COLS + MLA_COLS + DIL_COLS]

MLA_OUT = MLA_HEADS * MLA_V
DIL_OUT = DIL_HEADS * HEAD_DIM
DIFF_OUT = DIFF_HEADS * 2 * HEAD_DIM

kernel_name = 'hybrid_mla_dilated_diff_encoder'

def rms_norm(x, g):
    x32 = x.astype(jnp.float32)
    y = x32 * lax.rsqrt(jnp.mean(x32 * x32, axis=-1, keepdims=True) + NORM_EPS)
    return (y * g.astype(jnp.float32)).astype(x.dtype)

def rope_tables(positions, rot_dim):
    inv = ROPE_THETA ** (-jnp.arange(0, rot_dim, 2, dtype=jnp.float32) / rot_dim)
    ang = positions.astype(jnp.float32)[..., None] * inv
    return jnp.cos(ang), jnp.sin(ang)

def apply_rope(x, cos, sin):
    r = 2 * cos.shape[-1]
    shape = cos.shape[:2] + (1,) * (x.ndim - 3) + cos.shape[-1:]
    c = cos.reshape(shape)
    s = sin.reshape(shape)
    xr = x[..., :r].astype(jnp.float32)
    x1, x2 = xr[..., : r // 2], xr[..., r // 2:]
    rot = jnp.concatenate([x1 * c - x2 * s, x2 * c + x1 * s], axis=-1).astype(x.dtype)
    return jnp.concatenate([rot, x[..., r:]], axis=-1)

def blocked_softmax_attention(q, k, v, scale):
    B, S, H, dk = q.shape
    nq = S // QBLOCK
    qb = q.reshape(B, nq, QBLOCK, H, dk).transpose(1, 0, 2, 3, 4)

    def one(qblk):
        s = jnp.einsum('bqhd,bkhd->bhqk', qblk, k, preferred_element_type=jnp.float32) * scale
        p = jax.nn.softmax(s, axis=-1).astype(v.dtype)
        return jnp.einsum('bhqk,bkhd->bqhd', p, v)

    out = lax.map(one, qb)
    return out.transpose(1, 0, 2, 3, 4).reshape(B, S, H, v.shape[-1])

def blocked_diff_attention(q, k, v, lam, scale):
    B, S, H, _, dh = q.shape
    nq = S // QBLOCK
    qb = q.reshape(B, nq, QBLOCK, H, 2, dh).transpose(1, 0, 2, 3, 4, 5)

    def one(qblk):
        s = jnp.einsum('bqhmd,bkhmd->bhmqk', qblk, k, preferred_element_type=jnp.float32) * scale
        p = jax.nn.softmax(s, axis=-1)
        a = (p[:, :, 0] - lam * p[:, :, 1]).astype(v.dtype)
        return jnp.einsum('bhqk,bkhd->bqhd', a, v)

    out = lax.map(one, qb)
    return out.transpose(1, 0, 2, 3, 4).reshape(B, S, H, v.shape[-1])

def banded_attention(q, k, v, radius, scale):
    lead = q.shape[:-2]
    L, dh = q.shape[-2], q.shape[-1]
    blk = radius
    nb = -(-L // blk)
    lp = nb * blk
    nlead = len(lead)
    qb = jnp.pad(q, [(0, 0)] * nlead + [(0, lp - L), (0, 0)]).reshape(lead + (nb, blk, dh))

    def windows(t):
        tb = jnp.pad(t, [(0, 0)] * nlead + [(blk, lp - L + blk), (0, 0)])
        tb = tb.reshape(lead + (nb + 2, blk, t.shape[-1]))
        return jnp.concatenate([tb[..., :-2, :, :], tb[..., 1:-1, :, :], tb[..., 2:, :, :]], axis=-2)

    kw, vw = windows(k), windows(v)
    qpos = jnp.arange(lp).reshape(nb, blk, 1)
    kpos = (jnp.arange(nb)[:, None] * blk + jnp.arange(3 * blk)[None, :] - blk)[:, None, :]
    valid = (jnp.abs(qpos - kpos) <= radius) & (kpos >= 0) & (kpos < L)
    s = jnp.einsum('...nqd,...nkd->...nqk', qb, kw, preferred_element_type=jnp.float32) * scale
    s = jnp.where(valid, s, -jnp.inf)
    lse = jax.nn.logsumexp(s, axis=-1, keepdims=True)
    p = jnp.exp(s - lse).astype(v.dtype)
    o = jnp.einsum('...nqk,...nkd->...nqd', p, vw)
    o = o.reshape(lead + (lp, v.shape[-1]))[..., :L, :]
    lse = lse.reshape(lead + (lp,))[..., :L]
    return o, lse

def mla_mixer(mla_in, q_norm, w_uq, kv_norm, w_ukv, cos_m, sin_m):
    B, S, _ = mla_in.shape
    c_q, c_kv, k_rope = jnp.split(mla_in, [MLA_Q_RANK, MLA_Q_RANK + MLA_KV_RANK], axis=-1)
    q = (rms_norm(c_q, q_norm) @ w_uq).reshape(B, S, MLA_HEADS, MLA_NOPE + MLA_ROPE)
    q = jnp.concatenate([q[..., :MLA_NOPE], apply_rope(q[..., MLA_NOPE:], cos_m, sin_m)], axis=-1)
    kv = (rms_norm(c_kv, kv_norm) @ w_ukv).reshape(B, S, MLA_HEADS, MLA_NOPE + MLA_V)
    k_nope, v = kv[..., :MLA_NOPE], kv[..., MLA_NOPE:]
    k_rope = apply_rope(k_rope, cos_m, sin_m)
    k = jnp.concatenate([k_nope, jnp.broadcast_to(k_rope[:, :, None, :], (B, S, MLA_HEADS, MLA_ROPE))], axis=-1)
    o = blocked_softmax_attention(q, k, v, (MLA_NOPE + MLA_ROPE) ** -0.5)
    return o.reshape(B, S, MLA_OUT)

def dilated_mixer(dil_in, cos_p, sin_p):
    B, S, _ = dil_in.shape
    qkv = dil_in.reshape(B, S, DIL_GROUPS, 3, DIL_HEADS, HEAD_DIM)
    outs, lses = [], []
    for g, (window, dil) in enumerate(DIL_CONFIGS):
        q = apply_rope(qkv[:, :, g, 0], cos_p, sin_p)
        k = apply_rope(qkv[:, :, g, 1], cos_p, sin_p)
        v = qkv[:, :, g, 2]
        radius = window // (2 * dil)

        def to_sub(t):
            return t.reshape(B, S // dil, dil, DIL_HEADS, HEAD_DIM).transpose(0, 2, 3, 1, 4)

        o, lse = banded_attention(to_sub(q), to_sub(k), to_sub(v), radius, HEAD_DIM ** -0.5)
        outs.append(o.transpose(0, 3, 1, 2, 4).reshape(B, S, DIL_HEADS, HEAD_DIM))
        lses.append(lse.transpose(0, 3, 1, 2).reshape(B, S, DIL_HEADS))
    alpha = jax.nn.softmax(jnp.stack(lses, axis=0), axis=0)
    o = jnp.sum(alpha[..., None] * jnp.stack(outs, axis=0).astype(jnp.float32), axis=0)
    return o.astype(dil_in.dtype).reshape(B, S, DIL_OUT)

def diff_mixer(diff_in, lam_vecs, subln, lam_init, cos_p, sin_p):
    B, S, _ = diff_in.shape
    dq, dk, dv = jnp.split(diff_in, 3, axis=-1)
    dq = apply_rope(dq.reshape(B, S, DIFF_HEADS, 2, HEAD_DIM), cos_p, sin_p)
    dk = apply_rope(dk.reshape(B, S, DIFF_HEADS, 2, HEAD_DIM), cos_p, sin_p)
    dv = dv.reshape(B, S, DIFF_HEADS, 2 * HEAD_DIM)
    lv = lam_vecs.astype(jnp.float32)
    lam = jnp.exp(jnp.sum(lv[0] * lv[1])) - jnp.exp(jnp.sum(lv[2] * lv[3])) + lam_init
    o = blocked_diff_attention(dq, dk, dv, lam, HEAD_DIM ** -0.5)
    o = rms_norm(o, subln) * (1.0 - lam_init)
    return o.reshape(B, S, DIFF_OUT)

def conv_gated_mlp(h, w_up, conv_w, w_down):
    S = h.shape[1]
    u = h @ w_up
    pad = CONV_WIDTH // 2
    up = jnp.pad(u, ((0, 0), (pad, pad), (0, 0)))
    u = sum(up[:, t:t + S] * conv_w[t] for t in range(CONV_WIDTH))
    gate, val = jnp.split(u, 2, axis=-1)
    return (jax.nn.gelu(gate, approximate=True) * val) @ w_down

def lambda_init(layer):
    return 0.8 - 0.6 * math.exp(-0.3 * layer)

def setup_inputs(seed: int = 0) -> dict:
    key = jax.random.key(seed)
    ks = jax.random.split(key, 24)
    f32 = jnp.float32

    def nrm(k, shape, scale):
        return jax.random.normal(k, shape, f32) * scale

    def gain(k, n):
        return 1.0 + 0.02 * jax.random.normal(k, (DEPTH, n), f32)

    x = jax.random.normal(ks[0], (BATCH, SEQ, D_MODEL), f32)
    positions = jnp.arange(SEQ, dtype=jnp.int32)[None, :] + jax.random.randint(ks[1], (BATCH, 1), 0, 1024, dtype=jnp.int32)
    return {
        'x': x,
        'positions': positions,
        'attn_pre_norm': gain(ks[2], D_MODEL),
        'w_in': nrm(ks[3], (DEPTH, D_MODEL, IN_COLS), D_MODEL ** -0.5),
        'mla_q_norm': gain(ks[4], MLA_Q_RANK),
        'mla_w_uq': nrm(ks[5], (DEPTH, MLA_Q_RANK, MLA_HEADS * (MLA_NOPE + MLA_ROPE)), MLA_Q_RANK ** -0.5),
        'mla_kv_norm': gain(ks[6], MLA_KV_RANK),
        'mla_w_ukv': nrm(ks[7], (DEPTH, MLA_KV_RANK, MLA_HEADS * (MLA_NOPE + MLA_V)), MLA_KV_RANK ** -0.5),
        'diff_lambda': nrm(ks[8], (DEPTH, 4, HEAD_DIM), 0.1),
        'diff_subln': gain(ks[9], 2 * HEAD_DIM),
        'w_branch_mla': nrm(ks[10], (DEPTH, MLA_OUT, D_MODEL), MLA_OUT ** -0.5),
        'w_branch_dil': nrm(ks[11], (DEPTH, DIL_OUT, D_MODEL), DIL_OUT ** -0.5),
        'w_branch_diff': nrm(ks[12], (DEPTH, DIFF_OUT, D_MODEL), DIFF_OUT ** -0.5),
        'w_out': nrm(ks[13], (DEPTH, D_MODEL, D_MODEL), D_MODEL ** -0.5),
        'attn_post_norm': gain(ks[14], D_MODEL),
        'ffn_pre_norm': gain(ks[15], D_MODEL),
        'w_up': nrm(ks[16], (DEPTH, D_MODEL, 2 * D_FF), D_MODEL ** -0.5),
        'ffn_conv': nrm(ks[17], (DEPTH, CONV_WIDTH, 2 * D_FF), CONV_WIDTH ** -0.5),
        'w_down': nrm(ks[18], (DEPTH, D_FF, D_MODEL), D_FF ** -0.5),
        'ffn_post_norm': gain(ks[19], D_MODEL),
    }

def reference(x, positions, attn_pre_norm, w_in, mla_q_norm, mla_w_uq, mla_kv_norm, mla_w_ukv, diff_lambda, diff_subln, w_branch_mla, w_branch_dil, w_branch_diff, w_out, attn_post_norm, ffn_pre_norm, w_up, ffn_conv, w_down, ffn_post_norm):
    cos_p, sin_p = rope_tables(positions, PARTIAL_ROT_DIM)
    cos_m, sin_m = rope_tables(positions, MLA_ROPE)
    for l in range(DEPTH):
        h = rms_norm(x, attn_pre_norm[l])
        proj = jnp.einsum('bsd,dc->bsc', h, w_in[l])
        gates, mla_in, dil_in, diff_in = jnp.split(proj, SPLITS, axis=-1)
        o_mla = mla_mixer(mla_in, mla_q_norm[l], mla_w_uq[l], mla_kv_norm[l], mla_w_ukv[l], cos_m, sin_m)
        o_dil = dilated_mixer(dil_in, cos_p, sin_p)
        o_diff = diff_mixer(diff_in, diff_lambda[l], diff_subln[l], lambda_init(l), cos_p, sin_p)
        g_mla, g_dil, g_diff = jnp.split(jax.nn.sigmoid(gates), N_BRANCH, axis=-1)
        merged = g_mla * (o_mla @ w_branch_mla[l]) + g_dil * (o_dil @ w_branch_dil[l]) + g_diff * (o_diff @ w_branch_diff[l])
        x = x + rms_norm(merged @ w_out[l], attn_post_norm[l])
        h = rms_norm(x, ffn_pre_norm[l])
        x = x + rms_norm(conv_gated_mlp(h, w_up[l], ffn_conv[l], w_down[l]), ffn_post_norm[l])
    return x


_drawn_inputs = setup_inputs


def setup_inputs(seed=0):
    import zlib

    import numpy as np

    out = dict(_drawn_inputs(seed))
    spreads = {}
    factors = {'mla_q_norm': 8.0,
     'mla_kv_norm': 8.0,
     'ffn_post_norm': 3.623,
     'diff_lambda': 3.863,
     'diff_subln': 8.0}
    for name, (base, spread) in spreads.items():
        noise = np.random.default_rng([zlib.crc32(name.encode()), seed]).standard_normal(out[name].shape)
        drawn = base * np.exp(spread * noise) if base else spread * noise
        out[name] = __import__('jax').numpy.asarray(drawn.astype(out[name].dtype))
    for name, factor in factors.items():
        out[name] = (out[name] * factor).astype(out[name].dtype)
    return out
```

```python
from contextlib import ExitStack
import math

import numpy as np

import concourse.bass as bass
from concourse import mybir

F32 = mybir.dt.float32
F32R = mybir.dt.float32r
BF16 = mybir.dt.bfloat16
I32 = mybir.dt.int32
ALU = mybir.AluOpType
ACT = mybir.ActivationFunctionType
AX = mybir.AxisListType

P = 128
D = 1024
SEQ = 256
DEPTH = 2
NT = SEQ // P
KD = D // P
EPS = 1e-6

MLA_H, NOPE, ROPE, MLA_V = 8, 64, 32, 64
QK_M = NOPE + ROPE
Q_RANK, KV_RANK = 384, 256
MLA_COLS = Q_RANK + KV_RANK + ROPE
HD, ROT = 64, 16
DIL_G, DIL_H = 3, 6
DIFF_H = 4
D_FF = 2816
FT = D_FF // P
GATE0 = 0
MLA0 = 3 * D
DIL0 = MLA0 + MLA_COLS
DIFF0 = DIL0 + DIL_G * 3 * DIL_H * HD
MLA_SCALE = float(QK_M) ** -0.5
SCALE = float(HD) ** -0.5
MASKED = -(2.0 ** 100)

NB = 4
BASE = 1
RING = 3
NU = D_FF // 256


def plan_pieces():
    pieces = []
    for c in range(2):
        pieces += [("mla", c, k, 4, 336) for k in (0, 4)]
    pieces += [("diff", 0, k, 4, 512) for k in (0, 4)]
    pieces += [("uq", c, 0, 3, 384) for c in range(2)]
    pieces += [("ukv", c, 0, 2, 512) for c in range(2)]
    for c in (1, 2):
        pieces += [("diff", c, k, 4, 512) for k in (0, 4)]
    for c in range(9):
        pieces += [("dil", c, k, 4, 384) for k in (0, 4)]
    for c in range(6):
        pieces += [("gate", c, k, 4, 512) for k in (0, 4)]
    pieces += [("bmla", 0, 0, 2, 1024), ("bmla", 0, 2, 2, 1024)]
    pieces += [("bdiff", 0, 0, 2, 1024), ("bdiff", 0, 2, 2, 1024)]
    pieces += [("bdil", 0, 0, 2, 1024), ("bdil", 0, 2, 1, 1024)]
    for c in range(2):
        pieces += [("out", c, k, 4, 512) for k in (0, 4)]
    for u in range(NU + 1):
        if u < NU:
            pieces += [("up", 2 * u, 0, 8, 256), ("up", 2 * u + 1, 0, 8, 256)]
        if u > 0:
            pieces += [("down", u - 1, 0, 2, 1024)]
    return pieces


PIECES = plan_pieces()
NPIECE = len(PIECES)
assert NPIECE % RING == 0
K_TOTAL = {"mla": 8, "diff": 8, "uq": 3, "ukv": 2, "dil": 8, "gate": 8, "bmla": 4, "bdiff": 4, "bdil": 3, "out": 8}


def plan_steps():
    s = [("pre",), ("turn", "attn")]
    n = 0

    def w():
        nonlocal n
        s.append(("w", n))
        n += 1

    for _ in range(4):
        w()
    s.append(("latent",))
    w(), w()
    s.append(("turn", "latent"))
    for turned in ((), (0,), (1, 2), (3, 4), (5, 6), (7,), (8, 9), ()):
        for t in turned:
            s.append(("tq", t))
        w()
    s += [("tq", 10), ("tq", 11)]
    waiting = []
    for i in range(28):
        s.append(("score", i))
        if i >= 3 and i % 2 == 1:
            s.append(("pv", (i - 2) // 2))
        for _ in range(3 if i == 15 else 1):
            kind, c = PIECES[n][0:2]
            last = PIECES[n][2] == 4
            w()
            if waiting:
                s.append(("tq", waiting.pop(0)))
            if kind == "dil" and last and c % 3 < 2:
                first = 12 + 4 * (c // 3) + 2 * (c % 3)
                waiting += [first, first + 1]
        if i >= 1 and i - 1 not in (8, 10, 12, 14):
            s.append(("tp", i - 1))
        if i in (20, 21):
            s.append(("td", i - 20))
    assert not waiting
    s.append(("tp", 27))
    w(), w()
    s.append(("pv", 13))
    for _ in range(4):
        w()
    s.append(("turn", "merged"))
    for _ in range(4):
        w()
    s += [("post", "attn"), ("pre",), ("turn", "ffn")]
    while n < NPIECE:
        w()
    s.append(("post", "ffn"))
    return s


STEPS = plan_steps()

T_ORDER = [x for x in STEPS if x[0] in ("tq", "tp", "td")]
T_OF = {x: n for n, x in enumerate(T_ORDER)}
NTB = len(T_ORDER)


def plan_tiles():
    tiles, first = [], {}
    for n, (kind, c, k0, nk, cols) in enumerate(PIECES):
        if kind == "up" or (kind == "down" and c > 0):
            continue
        if k0:
            continue
        first[n] = len(tiles)
        halves = max(1, cols // 512) if cols == 1024 else 1
        for h in range(halves):
            for t in range(NT):
                tiles.append((kind, c, h, t))
    return tiles, first


TILES, FIRST_TILE = plan_tiles()
NTILE = len(TILES)
assert NTILE % NB == 0
BY_DVE = ("bmla", "bdiff", "bdil", "out", "down")


def emptied(n):
    who = "dve" if TILES[n][0] in BY_DVE else "act"
    if TILES[n][0] in ("out", "down"):
        while n + 1 < NTILE and TILES[n + 1][0] == TILES[n][0]:
            n += 1
    return who, sum(1 for x in TILES[:n + 1] if (x[0] in BY_DVE) == (who == "dve"))


GROUP_END = {}
for _n, _p in enumerate(PIECES):
    if _p[0] == "up" or (_p[0] == "down" and _p[1] < NU - 1):
        continue
    if _p[0] == "down" or _p[2] + _p[3] == K_TOTAL[_p[0]]:
        _m = max(m for m, x in enumerate(TILES) if x[0] == _p[0] and (_p[0] == "down" or x[1] == _p[1]))
        GROUP_END[_m] = _n
NFULL = NTILE - len(GROUP_END)

N_DVE = sum(1 for x in TILES if x[0] in BY_DVE)
N_ACT = NTILE - N_DVE

STAGED = [n for n, (kind, c, h, t) in enumerate(TILES)
          if kind in ("uq", "ukv") or (kind == "diff" and c < 2) or (kind == "dil" and c % 3 < 2)]
STAGE_OF = {n: s for s, n in enumerate(STAGED)}
NSTAGE = len(STAGED)
SRING = 4

TURN_BANKS = {"attn": [(0, 2), (2, 2), (4, 2), (6, 2)], "merged": [(0, 2), (2, 2), (4, 2), (6, 2)],
              "ffn": [(0, 2), (2, 2), (4, 2), (6, 2)], "latent": [(0, 2), (2, 2), (4, 1)]}
TURN_ORDER = ["attn", "latent", "merged", "ffn"]
TURN_BEFORE = {"attn": 0, "latent": 4, "merged": 7, "ffn": 11}
NTURN = 15

NPAR = 3 * FT * 2 + 22 + 1
PRE_A, PRE_F, G_Q, G_KV, G_SUB, LAM = 132, 140, 148, 151, 153, 154


def pieces_2pi():
    out, rest = [], 2 * math.pi
    for _ in range(3):
        e = math.floor(math.log2(rest))
        q = 2.0 ** (e - 7)
        c = math.floor(rest / q) * q
        out.append(c)
        rest -= c
    return out + [float(np.float32(rest))]


def lambda_init(layer):
    return 0.8 - 0.6 * math.exp(-0.3 * layer)


def build_trunk(nc, a, out):
    with ExitStack() as ctx:
        def sb(name, shape, dt=F32, scope=ctx):
            return scope.enter_context(nc.sbuf_tensor(name, shape, dt))

        def sem(name):
            return ctx.enter_context(nc.semaphore(name))

        x = sb("x_rows", [P, NT, D])
        hT_hi = sb("hT_hi", [P, KD, SEQ], F32R)
        hT_lo = sb("hT_lo", [P, KD, SEQ], F32R)
        raw = sb("w_raw", [P, RING, 2048])
        w_hi = sb("w_hi", [P, RING, 2048], F32R)
        w_lo = sb("w_lo", [P, RING, 2048], F32R)
        post_gain = sb("post_gain", [P, D])
        ident = sb("ident", [P, P])
        ident_b = sb("ident_b", [P, P], BF16)
        mask = sb("mask", [P, NT, 512], BF16)
        cosT = sb("cosT", [P, NT, 16])
        sinT = sb("sinT", [P, NT, 16])
        par_all = sb("par_all", [P, DEPTH, NPAR])
        par = sb("par", [P, NPAR])
        small = sb("small", [P, 64])
        rope_a = sb("rope_a", [P, 256])
        rope_b = sb("rope_b", [P, 256])

        with ExitStack() as one:
            diff_qT = sb("diff_qT", [P, 4, SEQ], scope=one)
            diff_kT = sb("diff_kT", [P, 4, SEQ], scope=one)
            mla_qT = sb("mla_qT", [P, MLA_H, SEQ], scope=one)
            mla_kT = sb("mla_kT", [P, MLA_H, SEQ], scope=one)
            mla_seq = sb("mla_seq", [P, NT, 704], scope=one)
            v_mla = sb("v_mla", [P, NT, MLA_H, MLA_V], scope=one)
            v_diff = sb("v_diff", [P, NT, 512], scope=one)
            sb("pad_gates", [P, 640], scope=one)
            dil_qT = sb("dil_qT", [P, 3, DIL_G, SEQ], scope=one)
            dil_kT = sb("dil_kT", [P, 3, DIL_G, SEQ], scope=one)
            v_dil = sb("v_dil", [P, NT, DIL_G, 384], scope=one)
            stage = sb("stage", [P, SRING, 512], scope=one)
            probs = sb("probs", [P, 2, 512], scope=one)
            probsT = sb("probsT", [P, 2, 4, SEQ], scope=one)
            diff_o = sb("diff_o", [P, NT, 512], scope=one)
        with ExitStack() as two:
            diff_oT = sb("diff_oT", [P, 2, 4, SEQ], F32R, scope=two)
            mla_oT = sb("mla_oT", [P, 4, 2, SEQ], F32R, scope=two)
            gates = sb("gates", [P, NT, 3 * D], scope=two)
            dil_oT = sb("dil_oT", [P, 3, 3, SEQ], F32R, scope=two)
            merged = sb("merged", [P, NT, D], scope=two)
            sb("pad_merged", [P, 256], scope=two)
            sb("pad_two", [P, NT * DIL_G * 384 + SRING * 512], scope=two)
            xn = sb("x_normed", [P, NT, D], scope=two)
        with ExitStack() as three:
            sb("pad_three", [P, 2 * 4 * SEQ + 4 * 2 * SEQ + NT * 3 * D], scope=three)
            latT_hi = sb("latT_hi", [P, 5, SEQ], F32R, scope=three)
            latT_lo = sb("latT_lo", [P, 5, SEQ], F32R, scope=three)
            sb("pad_three_b", [P, 2048 - 512], scope=three)
        with ExitStack() as four:
            conv = sb("conv_out", [P, 2, 2, 512], scope=four)
            g_hi = sb("g_hi", [P, 2, 512], F32R, scope=four)
            g_lo = sb("g_lo", [P, 2, 512], F32R, scope=four)
            square_ffn = sb("square_ffn", [P, D], scope=four)
            par_rows = sb("par_rows", [44, 7, P], scope=four)
            lam_rows = sb("lam_rows", [P, DEPTH, 4, HD], scope=four)
            pos_i = sb("pos_i", [P, NT], I32, scope=four)
            pos_f = sb("pos_f", [P, NT], scope=four)
            ang = sb("ang", [P, NT, 16], scope=four)
            turns = sb("turns", [P, NT, 16], scope=four)
            iot = sb("iot", [P, P], I32, scope=four)
            mod_f = sb("mod_f", [P, P], scope=four)
            inv_freq = sb("inv_freq", [P, 16], scope=four)
            lam_prod = sb("lam_prod", [P, DEPTH, 2, HD], scope=four)
            lam_sum = sb("lam_sum", [P, DEPTH, 2], scope=four)
            lam_exp = sb("lam_exp", [P, DEPTH, 2], scope=four)

        bank = [ctx.enter_context(nc.psum_tensor(f"bank{i}", [P, 512], F32)) for i in range(8)]
        S_BANK, T_BANK, O_BANK = (bank[4], bank[5]), bank[6], bank[7]

        ss = small[:, 0:8]
        y_c = small[:, 8:16]
        t_c = small[:, 16:24]
        h_c = small[:, 24:32]
        m_c = small[:, 32:40]
        negmax = small[:, 40:44]
        rowsum = small[:, 44:48]
        rinv = small[:, 48:52]
        rstd_x = small[:, 52:54]

        raw_landed = [sem(f"raw_landed{i}") for i in range(RING)]
        hi_done, lo_done, piece_used = sem("hi_done"), sem("lo_done"), sem("piece_used")
        tile_full, tile_emptied_act, tile_emptied_dve = sem("tile_full"), sem("tile_emptied_act"), sem("tile_emptied_dve")
        roped = sem("roped")
        turn_full, turn_hi, turn_emptied = sem("turn_full"), sem("turn_hi"), sem("turn_emptied")
        t_full, t_emptied = sem("t_full"), sem("t_emptied")
        score_full, max_done, exp_done, probs_ready = sem("score_full"), sem("max_done"), sem("exp_done"), sem("probs_ready")
        o_full, o_hi, o_emptied = sem("o_full"), sem("o_hi"), sem("o_emptied")
        diff_rows, diff_hi, diff_lo = sem("diff_rows"), sem("diff_hi"), sem("diff_lo")
        squares, rstd_done, xn_done = sem("squares"), sem("rstd_done"), sem("xn_done")
        lat_squares, lat_normed = sem("lat_squares"), sem("lat_normed")
        merged_ready = sem("merged_ready")
        post_squares, x_ready = sem("post_squares"), sem("x_ready")
        conv_mid, conv_done = sem("conv_mid"), sem("conv_done")
        gelu_done, g_ready, g_hi_done, g_lo_done = sem("gelu_done"), sem("g_ready"), sem("g_hi_done"), sem("g_lo_done")
        gain_landed = sem("gain_landed")
        x_landed = sem("x_landed")
        first_loads, consts, par_turned, angles, tables = sem("first_loads"), sem("consts"), sem("par_turned"), sem("angles"), sem("tables")
        lam_sums, lam_exps, setup_done = sem("lam_sums"), sem("lam_exps"), sem("setup_done")
        par_ready, out_landed = sem("par_ready"), sem("out_landed")
        freqs, slot_claimed, key_claimed = sem("freqs"), sem("slot_claimed"), sem("key_claimed")

        N_FIRST = 4 + 3 * DEPTH + 5 * DEPTH + 1

        def weight_source(l, kind, c, k0, nk, cols):
            if kind in ("mla", "diff", "dil", "gate"):
                c0 = {"mla": MLA0 + 336 * c, "diff": DIFF0 + 512 * c, "dil": DIL0 + 384 * c, "gate": 512 * c}[kind]
                src = a["w_in"]
            elif kind == "uq":
                src, c0 = a["mla_w_uq"], 384 * c
            elif kind == "ukv":
                src, c0 = a["mla_w_ukv"], 512 * c
            elif kind in ("bmla", "bdil", "bdiff"):
                src, c0 = a["w_branch_" + kind[1:]], 0
            elif kind == "out":
                src, c0 = a["w_out"], 512 * c
            elif kind == "up":
                src, c0 = a["w_up"], (c % 2) * D_FF + 256 * (c // 2)
            else:
                src, c0, k0 = a["w_down"], 0, 2 * c
            view = src.rearrange("l (k p) n -> l p k n", p=P)
            return view[l, :, k0:k0 + nk, c0:c0 + cols]

        def cut(buf, n):
            nk, cols = PIECES[n][3:5]
            return buf[:, n % RING, 0:nk * cols].rearrange("p (k n) -> p k n", k=nk)

        def own_order(cols):
            return cols.rearrange("p (j r) -> p r j", r=4)

        def by_class(cols):
            return cols.rearrange("p (r j) -> p r j", r=4)

        def own_order2(cols):
            return cols.rearrange("p (c j r) -> p c r j", c=2, r=4)

        def by_class2(cols):
            return cols.rearrange("p (c r j) -> p c r j", c=2, r=4)

        def class_rows(dram):
            view = dram[0].rearrange("(j r) d -> r j d", r=4)
            return [(slice(64 * (r % 2), 64 * (r % 2) + 64), r // 2, view[r]) for r in range(4)]

        def wait_tile(eng, l, m):
            if m in GROUP_END:
                eng.wait_ge(piece_used, l * NPIECE + (RING + GROUP_END[m] + 1))
            else:
                eng.wait_ge(tile_full, l * NFULL + (m + 1 - sum(1 for e in GROUP_END if e < m)))

        block = ctx.enter_context(nc.Block())

        @block.sync
        def _(sp):
            for part, t, src in class_rows(a["x"]):
                sp.dma_start(x[part, t, :], src).then_inc(x_landed, 16)
            with sp.Fori(0, DEPTH) as l:
                for n, piece in enumerate(PIECES):
                    sp.wait_ge(lo_done, l * NPIECE + (n + 1))
                    sp.sem_inc(slot_claimed, 1)
                    sp.dma_start(cut(raw, n), weight_source(l, *piece)).then_inc(raw_landed[n % RING], 16)
            sp.wait_ge(x_ready, BASE + 2 * NT * DEPTH)
            for part, t, dst in class_rows(out):
                sp.dma_start(dst, x[part, t, :]).then_inc(out_landed, 16)
            sp.wait_ge(out_landed, 16 * 4)

        @block.gpsimd
        def _(pool):
            positions = a["positions"][0, :].rearrange("(j r) -> j r", r=4)
            for r in range(4):
                h = 64 * (r % 2)
                pool.dma_start(pos_i[h:h + 64, r // 2:r // 2 + 1], positions[:, r:r + 1], allow_slow_non_contiguous=True).then_inc(first_loads, 16)
            for l in range(DEPTH):
                for tap in range(3):
                    pool.dma_start(par_rows[:, 3 * l + tap, :], a["ffn_conv"][l, tap, :].rearrange("(c p) -> c p", p=P)).then_inc(first_loads, 16)
                r0 = 22 * l
                for name, rows in (("attn_pre_norm", 8), ("ffn_pre_norm", 8), ("mla_q_norm", 3), ("mla_kv_norm", 2), ("diff_subln", 1)):
                    pool.dma_start(par_rows[r0:r0 + rows, 6, :], a[name][l, :].rearrange("(c p) -> c p", p=P)).then_inc(first_loads, 16)
                    r0 += rows
            pool.dma_start(lam_rows[:, :, :, :].rearrange("p l v d -> p (l v d)"),
                           a["diff_lambda"].rearrange("l v d -> (l v d)").partition_broadcast(P)).then_inc(first_loads, 16)
            inv = np.power(500000.0, -np.arange(0, ROPE, 2, dtype=np.float64) / ROPE).astype(np.float32)
            for k in range(16):
                nc.gpsimd.memset(inv_freq[:, k:k + 1], float(inv[k])).then_inc(freqs, 1)
            nc.gpsimd.memset(ident[:], 0.0)
            nc.gpsimd.memset(ident_b[:], 0.0)
            nc.gpsimd.memset(mask[:], 0.0)
            pool.drain()
            for m in (ident, ident_b):
                nc.gpsimd.affine_select(out=m[:], in_=m[:], compare_op=ALU.not_equal, fill=1.0, base=0,
                                        pattern=[[-1, P]], channel_multiplier=1)
            pool.drain()
            for t in range(NT):
                for h in range(2):
                    rq = 2 * t + h
                    m = mask[64 * h:64 * h + 64, t, 0:SEQ].rearrange("p (r j) -> p r j", r=4)
                    nc.gpsimd.affine_select(out=m, in_=m, compare_op=ALU.is_ge, fill=MASKED, base=rq + 64,
                                            pattern=[[-1, 4], [-4, 64]], channel_multiplier=4)
                    pool.drain()
                    nc.gpsimd.affine_select(out=m, in_=m, compare_op=ALU.is_ge, fill=MASKED, base=64 - rq,
                                            pattern=[[1, 4], [4, 64]], channel_multiplier=-4)
                    pool.drain()
            for t in range(NT):
                for g in range(2):
                    c0 = SEQ + P * g
                    nc.gpsimd.memset(mask[0:64, t, c0 + 64:c0 + 128], MASKED)
                    pool.drain()
                    nc.gpsimd.memset(mask[64:128, t, c0:c0 + 64], MASKED)
                    pool.drain()
            nc.gpsimd.iota(iot[:], pattern=[[-1, P]], base=P, channel_multiplier=1)
            pool.drain().then_inc(consts, 1)

            def rope(view, heads, first, half, t):
                step = 16 // half
                xr = view[:, :, first:first + 2 * half].rearrange("p h (s f) -> p h s f", s=2)
                shape = [P, heads, 2, half]
                c = cosT[:, t, ::step].rearrange("p (a b f) -> p a b f", a=1, b=1).broadcast_to(shape)
                s = sinT[:, t, ::step].rearrange("p (a b f) -> p a b f", a=1, b=1).broadcast_to(shape)
                n = heads * 2 * half
                ca = rope_a[:, 0:n].rearrange("p (h s f) -> p h s f", h=heads, s=2)
                sa = rope_b[:, 0:n].rearrange("p (h s f) -> p h s f", h=heads, s=2)
                nc.gpsimd.tensor_tensor(ca, xr, c, ALU.mult)
                nc.gpsimd.tensor_tensor(sa, xr, s, ALU.mult)
                pool.drain()
                nc.gpsimd.tensor_tensor(xr[:, :, 0, :], ca[:, :, 0, :], sa[:, :, 1, :], ALU.subtract)
                return nc.gpsimd.tensor_tensor(xr[:, :, 1, :], ca[:, :, 1, :], sa[:, :, 0, :], ALU.add)

            pool.wait_ge(tables, 1)
            with pool.Fori(0, DEPTH) as l:
                for n, (kind, c, half_no, t) in enumerate(TILES):
                    if kind == "mla" and c == 1:
                        pool.drain()
                        pool.wait_ge(tile_emptied_act, l * N_ACT + emptied(n)[1])
                        rope(mla_seq[:, t:t + 1, 640:672], 1, 0, 16, t)
                    if n not in STAGE_OF:
                        continue
                    pool.drain()
                    st = stage[:, STAGE_OF[n] % SRING, :]
                    pool.wait_ge(tile_emptied_act, l * N_ACT + emptied(n)[1])
                    if kind == "uq":
                        rope(st[:, 0:384].rearrange("p (h w) -> p h w", h=4), 4, NOPE, 16, t).then_inc(roped, 1)
                    elif kind == "ukv":
                        pool.sem_inc(key_claimed, 1)
                        kr = mla_seq[:, t:t + 1, 640:672].broadcast_to([P, 4, ROPE])
                        nc.gpsimd.tensor_copy(st[:, 0:384].rearrange("p (h w) -> p h w", h=4)[:, :, NOPE:QK_M], kr).then_inc(roped, 1)
                    elif kind == "diff":
                        rope(st.rearrange("p (h w) -> p h w", h=8), 8, 0, 8, t).then_inc(roped, 1)
                    else:
                        rope(st[:, 0:384].rearrange("p (h w) -> p h w", h=6), 6, 0, 8, t).then_inc(roped, 1)

        @block.scalar
        def _(act):
            act.sem_inc(t_emptied, BASE)
            act.wait_ge(angles, 1)
            nc.scalar.activation(sinT[:], ang[:], ACT.Sin)
            nc.scalar.activation(cosT[:], turns[:], ACT.Sin).then_inc(tables, 1)
            act.wait_ge(lam_sums, 1)
            nc.scalar.activation(lam_exp[:], lam_sum[:], ACT.Exp).then_inc(lam_exps, 1)
            act.wait_ge(setup_done, 1)

            def split_hi(l, n):
                nk, cols = PIECES[n][3:5]
                act.wait_ge(raw_landed[n % RING], (l * (NPIECE // RING) + (n // RING + 1)) * 16)
                act.wait_ge(piece_used, l * NPIECE + (n + 1))
                nc.scalar.activation(w_hi[:, n % RING, 0:nk * cols], raw[:, n % RING, 0:nk * cols], ACT.Copy).then_inc(hi_done, 1)

            def empty_tile(l, n):
                kind, c, h, t = TILES[n]
                src = bank[n % NB]
                wait_tile(act, l, n)
                if n in STAGE_OF:
                    s = STAGE_OF[n]
                    if s >= SRING:
                        act.wait_ge(t_full, l * NTB + (T_OF[("tq", s - SRING)] + 1))
                    dst = stage[:, s % SRING, :]
                    if kind == "uq" or kind == "dil":
                        last = nc.scalar.activation(dst[:, 0:384], src[:, 0:384], ACT.Copy)
                    elif kind == "diff":
                        last = nc.scalar.activation(dst, src[:], ACT.Copy)
                    else:
                        kv = src[:].rearrange("p (h w) -> p h w", h=4)
                        nc.scalar.activation(dst[:, 0:384].rearrange("p (h w) -> p h w", h=4)[:, :, 0:NOPE], kv[:, :, 0:NOPE], ACT.Copy)
                        last = nc.scalar.activation(v_mla[:, t, 4 * c:4 * c + 4, :], kv[:, :, NOPE:], ACT.Copy)
                elif kind == "mla":
                    last = nc.scalar.activation(mla_seq[:, t, 336 * c:336 * c + 336], src[:, 0:336], ACT.Copy)
                elif kind == "diff":
                    last = nc.scalar.activation(v_diff[:, t, :], src[:], ACT.Copy)
                elif kind == "dil":
                    last = nc.scalar.activation(v_dil[:, t, c // 3, :], src[:, 0:384], ACT.Copy)
                else:
                    last = nc.scalar.activation(gates[:, t, 512 * c:512 * c + 512], src[:], ACT.Tanh, scale=0.5)
                last.then_inc(tile_emptied_act, 1)

            def empty_t(l, key):
                n = T_OF[key]
                what, i = key
                act.wait_ge(t_full, l * NTB + (n + 1))
                if what == "tq":
                    kind, c, h, t = TILES[STAGED[i]]
                    rows = slice(t * P, (t + 1) * P)
                    if kind == "uq" or kind == "ukv":
                        dst = (mla_qT if kind == "uq" else mla_kT)[0:QK_M, 4 * c:4 * c + 4, rows]
                        nc.scalar.activation(dst, T_BANK[0:QK_M, :].rearrange("p (h q) -> p h q", h=4), ACT.Copy,
                                             scale=MLA_SCALE if kind == "uq" else 1.0).then_inc(t_emptied, 1)
                    elif kind == "diff":
                        dst = (diff_qT if c == 0 else diff_kT)[:, :, rows]
                        nc.scalar.activation(dst, T_BANK[:].rearrange("p (h q) -> p h q", h=4), ACT.Copy,
                                             scale=SCALE if c == 0 else 1.0).then_inc(t_emptied, 1)
                    else:
                        dst = (dil_qT if c % 3 == 0 else dil_kT)[:, :, c // 3, rows]
                        nc.scalar.activation(dst, T_BANK[:, 0:384].rearrange("p (h q) -> p h q", h=3), ACT.Copy,
                                             scale=SCALE if c % 3 == 0 else 1.0).then_inc(t_emptied, 1)
                elif what == "tp":
                    g, qt = i // 2, i % 2
                    if g >= 2:
                        act.wait_ge(o_full, l * 14 + (g - 1))
                    if 8 <= i < 16:
                        nc.scalar.activation(probsT[:, g % 2, 0:2, :].rearrange("p k (t q) -> p t k q", t=2),
                                             T_BANK[:].rearrange("p (t k q) -> p t k q", t=2, k=2), ACT.Copy).then_inc(t_emptied, 1)
                    else:
                        nc.scalar.activation(probsT[:, g % 2, :, qt * P:qt * P + P], T_BANK[:].rearrange("p (b q) -> p b q", b=4),
                                             ACT.Copy).then_inc(t_emptied, 1)
                else:
                    nc.scalar.activation(diff_o[:, i, :], T_BANK[:], ACT.Copy, scale=par[:, G_SUB:G_SUB + 1]).then_inc(t_emptied, 1)
                    act.wait_ge(t_emptied, BASE + l * NTB + (n + 1))
                    nc.scalar.activation(diff_oT[:, 0, :, i * P:i * P + P], diff_o[:, i, :].rearrange("p (h q) -> p h q", h=4),
                                         ACT.Copy).then_inc(diff_hi, 1)

            def empty_turn(l, what):
                for b, (k0, nk) in enumerate(TURN_BANKS[what]):
                    m = TURN_BEFORE[what] + b
                    act.wait_ge(turn_full, l * NTURN + (m + 1))
                    src = bank[4 + b]
                    if what == "merged":
                        last = nc.scalar.activation(hT_hi[:, k0:k0 + 2, :], src[:].rearrange("p (k q) -> p k q", k=2), ACT.Copy, scale=0.5)
                    else:
                        dst = latT_hi if what == "latent" else hT_hi
                        g0 = {"attn": PRE_A, "ffn": PRE_F, "latent": G_Q}[what]
                        for k in range(nk):
                            col, from_bank = dst[:, k0 + k, :], src[:, k * SEQ:(k + 1) * SEQ]
                            if what == "ffn":
                                col, from_bank = own_order(col), by_class(from_bank)
                            last = nc.scalar.activation(col, from_bank, ACT.Copy,
                                                        scale=par[:, g0 + k0 + k:g0 + k0 + k + 1])
                    last.then_inc(turn_hi, 1)

            def pre(l, which):
                for t in range(NT):
                    if which == 0:
                        if t == 0:
                            act.wait_ge(x_landed, 16 * 4)
                        if t == 0:
                            act.wait_ge(x_ready, BASE + l * (2 * NT))
                            act.dma_start(post_gain[:], a["attn_post_norm"][l, :].partition_broadcast(P)).then_inc(gain_landed, 16)
                        act.wait_ge(par_ready, l + 1)
                    else:
                        act.wait_ge(x_ready, BASE + l * (2 * NT) + (t + 1))
                        if t == NT - 1:
                            act.dma_start(post_gain[:], a["ffn_post_norm"][l, :].partition_broadcast(P)).then_inc(gain_landed, 16)
                    nc.scalar.activation(xn[:, t, :], x[:, t, :], ACT.Square, scale=1.0 / 32, accum_out=ss[:, t:t + 1]).then_inc(squares, 1)
                for t in range(NT):
                    act.wait_ge(rstd_done, l * (2 * NT) + (which * NT + t + 1))
                    nc.scalar.activation(xn[:, t, :], x[:, t, :], ACT.Copy, scale=rstd_x[:, t:t + 1]).then_inc(xn_done, 1)

            def post(l, which):
                first = NTILE - 4 if which else NTILE - 8
                for t in range(NT):
                    for h in range(2):
                        wait_tile(act, l, first + 2 * h + t)
                        nc.scalar.activation(xn[:, t, h * 512:h * 512 + 512],
                                             bank[2 * h + t][:], ACT.Square, scale=1.0 / 32,
                                             accum_out=ss[:, 4 + 2 * t + h:5 + 2 * t + h]).then_inc(post_squares, 1)

            with act.Fori(0, DEPTH) as l:
                split_hi(l, 0)
                split_hi(l, 1)
                done_pre = 0
                for step in STEPS:
                    what = step[0]
                    if what == "pre":
                        pre(l, done_pre)
                        done_pre += 1
                    elif what == "turn":
                        empty_turn(l, step[1])
                    elif what == "latent":
                        for t in range(NT):
                            act.wait_ge(tile_emptied_act, l * N_ACT + 4)
                            nc.scalar.activation(xn[:, t, 0:Q_RANK], mla_seq[:, t, 0:Q_RANK], ACT.Square,
                                                 accum_out=ss[:, 2 * t:2 * t + 1])
                            nc.scalar.activation(xn[:, t, 512:512 + KV_RANK], mla_seq[:, t, Q_RANK:Q_RANK + KV_RANK], ACT.Square,
                                                 accum_out=ss[:, 2 * t + 1:2 * t + 2]).then_inc(lat_squares, 1)
                    elif what in ("tq", "tp", "td"):
                        empty_t(l, step)
                    elif what == "score":
                        i = step[1]
                        act.wait_ge(max_done, l * 28 + (i + 1))
                        if 10 <= i <= 16 and i % 2 == 0:
                            act.wait_ge(probs_ready, l * 28 + i)
                        elif i >= 2:
                            act.wait_ge(t_full, l * NTB + (T_OF[("tp", i - 2)] + 1))
                        b = i % 2
                        if i < 16:
                            for h in range(2):
                                last = nc.scalar.activation(probs[:, b, h * SEQ:(h + 1) * SEQ], S_BANK[b][:, h * SEQ:(h + 1) * SEQ], ACT.Exp,
                                                            bias=negmax[:, 2 * b + h:2 * b + h + 1],
                                                            accum_out=rowsum[:, 2 * b + h:2 * b + h + 1])
                        else:
                            last = nc.scalar.activation(probs[:, b, :], S_BANK[b][:], ACT.Exp, bias=negmax[:, 2 * b:2 * b + 1],
                                                        accum_out=rowsum[:, 2 * b:2 * b + 1])
                        last.then_inc(exp_done, 1)
                    elif what == "pv":
                        g = step[1]
                        if g < 4 or g >= 8:
                            act.wait_ge(o_full, l * 14 + (g + 1))
                            if g < 4:
                                nc.scalar.activation(mla_oT[:, g, 0, :], O_BANK[:, 0:SEQ], ACT.Copy).then_inc(o_hi, 1)
                            elif g % 2 == 1:
                                nc.scalar.activation(dil_oT[:, (g - 8) // 2, 0, :], O_BANK[:, 0:SEQ], ACT.Copy).then_inc(o_hi, 1)
                    elif what == "post":
                        post(l, step[1] == "ffn")
                    elif what == "w":
                        n = step[1]
                        kind, c, k0, nk, cols = PIECES[n]
                        if n + 2 < NPIECE:
                            split_hi(l, n + 2)
                        if kind == "up":
                            u, b = c // 2, c % 2
                            act.wait_ge(piece_used, l * NPIECE + (RING + n + 1))
                            if u >= 2:
                                act.wait_ge(g_lo_done, l * NU + (u - 1))
                            for j in range(2):
                                ch = 22 * b + 2 * u + j
                                last = nc.scalar.activation(conv[:, u % 2, b, j * SEQ:(j + 1) * SEQ],
                                                            bank[4 + c % 4][:, j * SEQ:(j + 1) * SEQ], ACT.Copy,
                                                            scale=par[:, 44 + ch:45 + ch])
                            last.then_inc(conv_mid, 1)
                            if c % 2 == 1:
                                act.wait_ge(conv_done, BASE + l * 2 * NU + c)
                                nc.scalar.activation(conv[:, u % 2, 0, :], conv[:, u % 2, 0, :], ACT.Gelu_apprx_tanh).then_inc(gelu_done, 1)
                                act.wait_ge(g_ready, l * NU + (u + 1))
                                if u >= 2:
                                    act.wait_ge(piece_used, l * NPIECE + (RING + PIECES.index(("down", u - 2, 0, 2, 1024)) + 1))
                                nc.scalar.activation(by_class2(g_hi[:, u % 2, :]), own_order2(conv[:, u % 2, 1, :]), ACT.Copy).then_inc(g_hi_done, 1)
                        elif kind != "down" and k0 + nk == K_TOTAL[kind] and kind not in BY_DVE:
                            f = first_of(n)
                            for m in range(f, f + tiles_of(n)):
                                empty_tile(l, m)

        @block.vector
        def _(dve):
            V = nc.vector

            def newton(k, ms):
                y, t, h = y_c[:, 0:k], t_c[:, 0:k], h_c[:, 0:k]
                V.tensor_scalar(h, ms, -0.5, None, ALU.mult)
                V.tensor_scalar(t.bitcast(I32), ms.bitcast(I32), 1, None, ALU.logical_shift_right)
                dve.drain()
                V.tensor_scalar(y.bitcast(I32), t.bitcast(I32), -1.0, float(0x5F3759DF), ALU.mult, ALU.add)
                dve.drain()
                for _ in range(4):
                    if k == 1:
                        V.scalar_tensor_tensor(out=t, in0=y, scalar=h, in1=y, op0=ALU.mult, op1=ALU.mult)
                    else:
                        V.tensor_tensor(t, y, y, ALU.mult)
                        dve.drain()
                        V.tensor_tensor(t, t, h, ALU.mult)
                    dve.drain()
                    V.scalar_tensor_tensor(out=y, in0=t, scalar=1.5, in1=y, op0=ALU.add, op1=ALU.mult)
                    dve.drain()

            V.sem_inc(lo_done, RING)
            for started in (x_ready, tile_emptied_dve, conv_done, o_emptied):
                V.sem_inc(started, BASE)
            dve.wait_ge(first_loads, 16 * N_FIRST)
            dve.wait_ge(freqs, 16)
            V.tensor_copy(pos_f[:], pos_i[:])
            dve.drain()
            shape = [P, NT, 16]
            V.tensor_tensor(ang[:], pos_f[:].rearrange("p (a o) -> p a o", o=1).broadcast_to(shape),
                            inv_freq[:].rearrange("p (o f) -> p o f", o=1).broadcast_to(shape), ALU.mult)
            dve.drain()
            magic = 1.5 * 2.0 ** 23
            V.tensor_scalar(turns[:], ang[:], 1.0 / (2 * math.pi), None, ALU.mult)
            dve.drain()
            V.tensor_scalar(turns[:], turns[:], magic, None, ALU.add)
            dve.drain()
            V.tensor_scalar(turns[:], turns[:], -magic, None, ALU.add)
            dve.drain()
            for part in pieces_2pi():
                V.scalar_tensor_tensor(out=ang[:], in0=turns[:], scalar=-part, in1=ang[:], op0=ALU.mult, op1=ALU.add)
                dve.drain()
            top = float(np.float32(3.1415925))
            V.tensor_scalar(ang[:], ang[:], top, -top, ALU.min, ALU.max)
            dve.drain()
            V.tensor_scalar(turns[:], ang[:], -1.0, None, ALU.mult)
            dve.drain()
            V.tensor_tensor(turns[:], turns[:], ang[:], ALU.min)
            dve.drain()
            V.tensor_scalar(turns[:], turns[:], math.pi / 2, None, ALU.add).then_inc(angles, 1)
            V.tensor_tensor(lam_prod[:], lam_rows[:, :, 0:4:2, :], lam_rows[:, :, 1:4:2, :], ALU.mult)
            dve.drain()
            V.tensor_reduce(lam_sum[:], lam_prod[:], AX.X, ALU.add).then_inc(lam_sums, 1)
            dve.wait_ge(consts, 1)
            V.tensor_scalar(iot[:], iot[:], 3, None, ALU.bitwise_and)
            dve.drain()
            V.tensor_copy(mod_f[:], iot[:])
            dve.drain()
            V.tensor_scalar(mod_f[:], mod_f[:], 0.0, MASKED, ALU.is_gt, ALU.mult)
            dve.drain()
            for t in range(NT):
                V.tensor_tensor(mask[:, t, 384:512], mask[:, t, 384:512], mod_f[:], ALU.min)
            dve.wait_ge(par_turned, 1)
            for l in range(DEPTH):
                V.tensor_copy(par_all[:, l, 0:132], bank[6][:, 132 * l:132 * l + 132])
                V.tensor_copy(par_all[:, l, 132:154], bank[6][:, 264 + 22 * l:264 + 22 * l + 22])
            dve.drain()
            dve.wait_ge(lam_exps, 1)
            for l in range(DEPTH):
                V.tensor_scalar(par_all[:, l, G_SUB:G_SUB + 1], par_all[:, l, G_SUB:G_SUB + 1], 1.0 - lambda_init(l), None, ALU.mult)
                V.tensor_scalar(par_all[:, l, LAM:LAM + 1], lam_exp[:, l, 1:2], lam_exp[:, l, 0:1], -lambda_init(l), ALU.subtract, ALU.add)
            dve.drain().then_inc(setup_done, 1)
            def split_lo(l, n):
                nk, cols = PIECES[n][3:5]
                s = slice(0, nk * cols)
                dve.wait_ge(hi_done, l * NPIECE + (n + 1))
                V.tensor_tensor(w_lo[:, n % RING, s], raw[:, n % RING, s], w_hi[:, n % RING, s].bitcast(F32), ALU.subtract).then_inc(lo_done, 1)

            def empty_turn(l, what):
                for b, (k0, nk) in enumerate(TURN_BANKS[what]):
                    m = TURN_BEFORE[what] + b
                    dve.wait_ge(turn_hi, l * NTURN + (m + 1))
                    src = bank[4 + b]
                    if what == "merged":
                        last = V.scalar_tensor_tensor(out=hT_lo[:, k0:k0 + 2, :], in0=src[:].rearrange("p (k q) -> p k q", k=2), scalar=0.5,
                                                      in1=hT_hi[:, k0:k0 + 2, :].bitcast(F32), op0=ALU.mult, op1=ALU.subtract)
                    else:
                        hi, lo = (latT_hi, latT_lo) if what == "latent" else (hT_hi, hT_lo)
                        g0 = {"attn": PRE_A, "ffn": PRE_F, "latent": G_Q}[what]
                        for k in range(nk):
                            lo_k, hi_k, from_bank = lo[:, k0 + k, :], hi[:, k0 + k, :].bitcast(F32), src[:, k * SEQ:(k + 1) * SEQ]
                            if what == "ffn":
                                lo_k, hi_k, from_bank = own_order(lo_k), own_order(hi_k), by_class(from_bank)
                            last = V.scalar_tensor_tensor(out=lo_k, in0=from_bank, scalar=par[:, g0 + k0 + k:g0 + k0 + k + 1],
                                                          in1=hi_k, op0=ALU.mult, op1=ALU.subtract)
                    last.then_inc(turn_emptied, 1)

            def negmax_of(l, i):
                b = i % 2
                dve.wait_ge(score_full, l * 28 + (i + 1))
                if i < 16:
                    V.tensor_reduce(negmax[:, 2 * b:2 * b + 2], S_BANK[b][:].rearrange("p (h k) -> p h k", h=2), AX.X, ALU.max,
                                    negate=True).then_inc(max_done, 1)
                else:
                    V.tensor_reduce(negmax[:, 2 * b:2 * b + 1], S_BANK[b][:], AX.X, ALU.max, negate=True).then_inc(max_done, 1)

            def normalise(l, i):
                b = i % 2
                dve.wait_ge(exp_done, l * 28 + (i + 1))
                w = 2 if i < 16 else 1
                V.reciprocal(rinv[:, 2 * b:2 * b + w], rowsum[:, 2 * b:2 * b + w])
                dve.drain()
                if i < 8:
                    for h in range(2):
                        s = slice(h * SEQ, (h + 1) * SEQ)
                        last = V.tensor_scalar(probs[:, b, s], probs[:, b, s], rinv[:, 2 * b + h:2 * b + h + 1], None, ALU.mult)
                elif i < 16 and b == 0:
                    for t in range(NT):
                        s = slice(t * SEQ, (t + 1) * SEQ)
                        last = V.tensor_scalar(probs[:, 0, s], probs[:, 0, s], rinv[:, t:t + 1], None, ALU.mult)
                elif i < 16:
                    V.tensor_scalar(rinv[:, 2:4], rinv[:, 2:4], par[:, LAM:LAM + 1], None, ALU.mult)
                    dve.drain()
                    for t in range(NT):
                        s = slice(t * SEQ, (t + 1) * SEQ)
                        last = V.scalar_tensor_tensor(out=probs[:, 1, s], in0=probs[:, 1, s], scalar=rinv[:, 2 + t:3 + t],
                                                      in1=probs[:, 0, s], op0=ALU.mult, op1=ALU.add)
                else:
                    last = V.tensor_scalar(probs[:, b, :], probs[:, b, :], rinv[:, 2 * b:2 * b + 1], None, ALU.mult)
                last.then_inc(probs_ready, 1)

            def empty_o(l, g):
                if g < 4:
                    dve.wait_ge(o_hi, l * 7 + (g + 1))
                    V.tensor_tensor(mla_oT[:, g, 1, :], O_BANK[:, 0:SEQ], mla_oT[:, g, 0, :].bitcast(F32), ALU.subtract).then_inc(o_emptied, 1)
                elif g < 8:
                    dve.wait_ge(o_full, l * 14 + (g + 1))
                    h = g - 4
                    V.tensor_copy(diff_o[:, :, h * P:(h + 1) * P], O_BANK[:, 0:SEQ].rearrange("p (t d) -> p t d", t=2)).then_inc(o_emptied, 1)
                elif g % 2 == 1:
                    pair = (g - 8) // 2
                    dve.wait_ge(o_hi, l * 7 + (5 + pair))
                    V.tensor_tensor(dil_oT[:, pair, 1, :], O_BANK[:, 0:SEQ], dil_oT[:, pair, 0, :].bitcast(F32), ALU.subtract).then_inc(o_emptied, 1)
                if g == 7:
                    dve.drain()
                    for t in range(NT):
                        V.tensor_tensor(head_squares(t), diff_o[:, t, :], diff_o[:, t, :], ALU.mult)
                        dve.drain()
                        V.tensor_reduce(ss[:, 4 * t:4 * t + 4], head_squares(t).rearrange("p (h d) -> p h d", h=4), AX.X, ALU.add)
                    dve.drain()
                    V.tensor_scalar(m_c[:, 0:8], ss[:, 0:8], 1.0 / P, EPS, ALU.mult, ALU.add)
                    dve.drain()
                    newton(8, m_c[:, 0:8])
                    for t in range(NT):
                        rows = diff_o[:, t, :].rearrange("p (h d) -> p h d", h=4)
                        V.tensor_tensor(rows, rows, y_c[:, 4 * t:4 * t + 4].rearrange("p (h o) -> p h o", o=1).broadcast_to([P, 4, P]),
                                        ALU.mult).then_inc(diff_rows, 1)

            def head_squares(t):
                return stage[:, t, :]

            def pre(l, which):
                for t in range(NT):
                    dve.wait_ge(squares, l * (2 * NT) + (which * NT + t + 1))
                    V.tensor_scalar(m_c[:, 0:1], ss[:, t:t + 1], EPS, None, ALU.add)
                    dve.drain()
                    newton(1, m_c[:, 0:1])
                    V.tensor_copy(rstd_x[:, t:t + 1], y_c[:, 0:1]).then_inc(rstd_done, 1)

            def post(l, which):
                first = NTILE - 4 if which else NTILE - 8
                dve.wait_ge(gain_landed, (l * 2 + (which + 1)) * 16)
                for t in range(NT):
                    dve.wait_ge(post_squares, l * 8 + (which * 4 + 2 * t + 2))
                    V.tensor_scalar(m_c[:, 0:1], ss[:, 4 + 2 * t:5 + 2 * t], ss[:, 5 + 2 * t:6 + 2 * t], EPS, ALU.add, ALU.add)
                    dve.drain()
                    newton(1, m_c[:, 0:1])
                    for h in range(2):
                        s = slice(h * 512, h * 512 + 512)
                        V.scalar_tensor_tensor(out=post_tmp(which, t)[:, s], in0=bank[2 * h + t][:], scalar=y_c[:, 0:1], in1=post_gain[:, s],
                                               op0=ALU.mult, op1=ALU.mult).then_inc(tile_emptied_dve, 1)
                    dve.drain()
                    V.tensor_tensor(x[:, t, :], x[:, t, :], post_tmp(which, t), ALU.add).then_inc(x_ready, 1)

            def post_tmp(which, t):
                return square_ffn[:] if which else merged[:, t, :]

            with dve.Fori(0, DEPTH) as l:
                dve.drain()
                V.tensor_copy(par[:], par_all[:, l, :]).then_inc(par_ready, 1)
                dve.drain()
                done_pre = 0
                for step in STEPS:
                    what = step[0]
                    if what == "pre":
                        pre(l, done_pre)
                        if done_pre == 0:
                            split_lo(l, 0)
                            split_lo(l, 1)
                        done_pre += 1
                    elif what == "turn":
                        empty_turn(l, step[1])
                    elif what == "latent":
                        dve.wait_ge(lat_squares, l * 2 + 2)
                        V.tensor_scalar(m_c[:, 0:4:2], ss[:, 0:4:2], 1.0 / Q_RANK, EPS, ALU.mult, ALU.add)
                        V.tensor_scalar(m_c[:, 1:4:2], ss[:, 1:4:2], 1.0 / KV_RANK, EPS, ALU.mult, ALU.add)
                        dve.drain()
                        newton(4, m_c[:, 0:4])
                        for t in range(NT):
                            for j, (c0, n) in enumerate(((0, Q_RANK), (Q_RANK, KV_RANK))):
                                last = V.tensor_scalar(mla_seq[:, t, c0:c0 + n], mla_seq[:, t, c0:c0 + n], y_c[:, 2 * t + j:2 * t + j + 1], None, ALU.mult)
                        last.then_inc(lat_normed, 1)
                    elif what == "score":
                        negmax_of(l, step[1])
                        normalise(l, step[1])
                    elif what == "pv":
                        empty_o(l, step[1])
                    elif what == "td":
                        t = step[1]
                        dve.wait_ge(diff_hi, l * 2 + (t + 1))
                        V.tensor_tensor(diff_oT[:, 1, :, t * P:t * P + P], diff_o[:, t, :].rearrange("p (h q) -> p h q", h=4),
                                        diff_oT[:, 0, :, t * P:t * P + P].bitcast(F32), ALU.subtract).then_inc(diff_lo, 1)
                    elif what == "post":
                        post(l, 1 if step[1] == "ffn" else 0)
                    elif what == "w":
                        n = step[1]
                        kind, c, k0, nk, cols = PIECES[n]
                        if n + 2 < NPIECE:
                            split_lo(l, n + 2)
                        if kind in ("bmla", "bdiff", "bdil") and k0 + nk == K_TOTAL[kind]:
                            f = first_of(n)
                            for m in range(f, f + 4):
                                _, _, h, t = TILES[m]
                                s = slice(h * 512, h * 512 + 512)
                                g0 = {"bmla": 0, "bdil": D, "bdiff": 2 * D}[kind] + h * 512
                                wait_tile(dve, l, m)
                                if kind == "bmla":
                                    V.scalar_tensor_tensor(out=merged[:, t, s], in0=gates[:, t, g0:g0 + 512], scalar=1.0, in1=bank[m % NB][:],
                                                           op0=ALU.add, op1=ALU.mult).then_inc(tile_emptied_dve, 1)
                                else:
                                    gs = gates[:, t, g0:g0 + 512]
                                    V.scalar_tensor_tensor(out=gs, in0=gs, scalar=1.0, in1=bank[m % NB][:],
                                                           op0=ALU.add, op1=ALU.mult).then_inc(tile_emptied_dve, 1)
                                    dve.drain()
                                    last = V.tensor_tensor(merged[:, t, s], merged[:, t, s], gs, ALU.add)
                                    if kind == "bdil":
                                        last.then_inc(merged_ready, 1)
                        elif kind == "up":
                            u, b = c // 2, c % 2
                            dve.wait_ge(conv_mid, l * 2 * NU + (c + 1))
                            for j in range(2):
                                ch = 22 * b + 2 * u + j
                                o = j * SEQ
                                cv, src = conv[:, u % 2, b, :], bank[4 + c % 4]
                                V.scalar_tensor_tensor(out=cv[:, o + 1:o + SEQ], in0=src[:, o:o + SEQ - 1], scalar=par[:, ch:ch + 1],
                                                       in1=cv[:, o + 1:o + SEQ], op0=ALU.mult, op1=ALU.add)
                            dve.drain()
                            for j in range(2):
                                ch = 22 * b + 2 * u + j
                                o = j * SEQ
                                last = V.scalar_tensor_tensor(out=cv[:, o:o + SEQ - 1], in0=src[:, o + 1:o + SEQ], scalar=par[:, 88 + ch:89 + ch],
                                                              in1=cv[:, o:o + SEQ - 1], op0=ALU.mult, op1=ALU.add)
                            last.then_inc(conv_done, 1)
                            if c % 2 == 1:
                                dve.drain()
                                dve.wait_ge(gelu_done, l * NU + (u + 1))
                                V.tensor_tensor(conv[:, u % 2, 1, :], conv[:, u % 2, 1, :], conv[:, u % 2, 0, :], ALU.mult).then_inc(g_ready, 1)
                                dve.wait_ge(g_hi_done, l * NU + (u + 1))
                                V.tensor_tensor(by_class2(g_lo[:, u % 2, :]), own_order2(conv[:, u % 2, 1, :]),
                                                by_class2(g_hi[:, u % 2, :].bitcast(F32)), ALU.subtract).then_inc(g_lo_done, 1)

        @block.tensor
        def _(pe):
            PE = nc.tensor
            pe.sem_inc(piece_used, RING)
            pe.wait_ge(consts, 1)
            pe.wait_ge(first_loads, 16 * N_FIRST)
            for j in range(7):
                last = PE.transpose(bank[6][:, 44 * j:44 * j + 44], par_rows[:, j, :], ident[0:44, 0:44])
            last.then_inc(par_turned, 1)
            pe.wait_ge(setup_done, 1)

            def passes(dst, lhs, rhs_hi, rhs_lo, start, stop):
                PE.matmul(dst, lhs[1], rhs_hi, start=start, stop=False)
                PE.matmul(dst, lhs[0], rhs_lo, start=False, stop=False)
                return PE.matmul(dst, lhs[0], rhs_hi, start=False, stop=stop)

            def rows(hi, lo, k, t):
                return hi[:, k, t * P:(t + 1) * P], lo[:, k, t * P:(t + 1) * P]

            def lhs_of(kind, c, k, t):
                if kind in ("mla", "diff", "dil", "gate", "out"):
                    return rows(hT_hi, hT_lo, k, t)
                if kind == "uq":
                    return rows(latT_hi, latT_lo, k, t)
                if kind == "ukv":
                    return rows(latT_hi, latT_lo, 3 + k, t)
                if kind == "bmla":
                    return mla_oT[:, k, 0, t * P:(t + 1) * P], mla_oT[:, k, 1, t * P:(t + 1) * P]
                if kind == "bmla" or kind == "bdil":
                    pe.wait_ge(o_emptied, BASE + l * 11 + (4 if kind == "bmla" else 11))
                if kind == "bdiff":
                    return diff_oT[:, 0, k, t * P:(t + 1) * P], diff_oT[:, 1, k, t * P:(t + 1) * P]
                if kind == "bdil":
                    return dil_oT[:, k, 0, t * P:(t + 1) * P], dil_oT[:, k, 1, t * P:(t + 1) * P]
                u = c
                return g_hi[:, u % 2, k * SEQ + t * P:k * SEQ + t * P + P], g_lo[:, u % 2, k * SEQ + t * P:k * SEQ + t * P + P]

            def wait_turned(l, kind, c, k):
                what = {"mla": "attn", "uq": "latent", "ukv": "latent", "out": "merged", "up": "ffn"}.get(kind)
                if what is None or c != 0:
                    return
                kk = k + 3 if kind == "ukv" else k
                pe.wait_ge(turn_emptied, l * NTURN + (TURN_BEFORE[what] + kk // 2 + 1))

            def use_piece(l, n):
                kind, c, k0, nk, cols = PIECES[n]
                hi, lo = cut(w_hi, n), cut(w_lo, n)
                pe.wait_ge(lo_done, l * NPIECE + (n + 1 + RING))
                if kind == "up":
                    u, b = c // 2, c % 2
                    if c >= 4:
                        pe.wait_ge(conv_done, BASE + l * 2 * NU + (c - 3))
                    for j in range(2):
                        for k in range(8):
                            if j == 0:
                                wait_turned(l, kind, c, k)
                            last = passes(bank[4 + c % 4][:, j * SEQ:(j + 1) * SEQ],
                                          (hi[:, k, j * P:(j + 1) * P], lo[:, k, j * P:(j + 1) * P]),
                                          hT_hi[:, k, :], hT_lo[:, k, :], k == 0, k == 7)
                    last.then_inc(piece_used, 1)
                    return
                halves = 2 if cols == 1024 else 1
                width = cols // halves
                if kind == "down":
                    f = NTILE - 4
                    pe.wait_ge(g_lo_done, l * NU + (c + 1))
                    start, stop = c == 0, c == NU - 1
                else:
                    f = first_of(n)
                    start, stop = k0 == 0, k0 + nk == K_TOTAL[kind]
                if kind == "bmla" or kind == "bdil":
                    pe.wait_ge(o_emptied, BASE + l * 11 + (4 if kind == "bmla" else 11))
                if kind == "bdiff":
                    pe.wait_ge(diff_lo, l * 2 + 2)
                for h in range(halves):
                    for t in range(NT):
                        m = f + 2 * h + t
                        if start:
                            if m >= NB:
                                who, count = emptied(m - NB)
                                if who == "act":
                                    pe.wait_ge(tile_emptied_act, l * N_ACT + count)
                                else:
                                    pe.wait_ge(tile_emptied_dve, BASE + l * N_DVE + count)
                            else:
                                pe.wait_ge(tile_emptied_dve, BASE + l * N_DVE + 0)
                        for k in range(nk):
                            kk = k if kind == "down" else k0 + k
                            if h == 0 and t == 0:
                                wait_turned(l, kind, c, kk)
                            last = passes(bank[m % NB][:, 0:width], lhs_of(kind, c, kk, t),
                                          hi[:, k, h * 512:h * 512 + width], lo[:, k, h * 512:h * 512 + width],
                                          start and k == 0, stop and k == nk - 1)
                        if stop and m not in GROUP_END:
                            last.then_inc(tile_full, 1)
                last.then_inc(piece_used, 1)

            def turn(l, what):
                before = TURN_BEFORE[what]
                for b, (k0, nk) in enumerate(TURN_BANKS[what]):
                    for k in range(nk):
                        for t in range(NT):
                            if b == 0 and k == 0:
                                if what == "attn":
                                    pe.wait_ge(xn_done, l * 2 * NT + (t + 1))
                                elif what == "ffn":
                                    pe.wait_ge(xn_done, l * 2 * NT + (NT + t + 1))
                                elif what == "latent":
                                    pe.wait_ge(lat_normed, l + 1)
                                else:
                                    pe.wait_ge(merged_ready, l * 4 + 4)
                                if t == 0:
                                    if what == "attn":
                                        pe.wait_ge(conv_done, BASE + l * 2 * NU)
                                    else:
                                        pe.wait_ge(turn_emptied, l * NTURN + before)
                                    if what == "merged":
                                        pe.wait_ge(o_emptied, BASE + l * 11 + 11)
                                        pe.wait_ge(t_emptied, BASE + l * NTB + NTB)
                            if what == "latent":
                                src = mla_seq[:, t, (k0 + k) * P:(k0 + k + 1) * P]
                            else:
                                src = (merged if what == "merged" else xn)[:, t, (k0 + k) * P:(k0 + k + 1) * P]
                            last = PE.transpose(bank[4 + b][:, k * SEQ + t * P:k * SEQ + t * P + P], src, ident[:])
                    last.then_inc(turn_full, 1)

            def wait_t(l, key):
                n = T_OF[key]
                pe.wait_ge(t_emptied, BASE + l * NTB + n)
                if key == ("tq", 0):
                    pe.wait_ge(turn_emptied, l * NTURN + 7)

            def scores(l, i):
                b = S_BANK[i % 2]
                qt = i % 2
                q = slice(qt * P, qt * P + P)
                if i >= 2:
                    pe.wait_ge(exp_done, l * 28 + (i - 1))
                if i < 8:
                    pair = i // 2
                    for h in range(2):
                        last = PE.matmul(b[:, h * SEQ:(h + 1) * SEQ], mla_qT[0:QK_M, 2 * pair + h, q], mla_kT[0:QK_M, 2 * pair + h, :], start=True, stop=True)
                elif i < 16:
                    head, m = i // 2 - 4, i % 2
                    r = slice(64 * m, 64 * m + 64)
                    for t in range(NT):
                        last = PE.matmul(b[:, t * SEQ:(t + 1) * SEQ], diff_qT[r, head, t * P:(t + 1) * P], diff_kT[r, head, :], start=True, stop=True)
                else:
                    head = i // 2 - 8
                    r = slice(64 * (head % 2), 64 * (head % 2) + 64)
                    PE.matmul(b[:], ident_b[:], mask[:, qt, :], start=True, stop=False, skip_group_check=True)
                    PE.matmul(b[:, 0:SEQ], dil_qT[r, head // 2, 0, q], dil_kT[r, head // 2, 0, :], start=False, stop=True, skip_group_check=True)
                    for g in (1, 2):
                        last = PE.matmul(b[:, P + g * P:2 * P + g * P], dil_qT[r, head // 2, g, q], dil_kT[r, head // 2, g, q],
                                         start=False, stop=True, skip_group_check=True)
                last.then_inc(score_full, 1)

            def products(l, g):
                pt = probsT[:, g % 2, :, :]
                pe.wait_ge(t_emptied, BASE + l * NTB + (T_OF[("tp", 2 * g + 1)] + 1))
                done = g if g <= 8 else 8 + (g - 8) // 2
                if g == 0:
                    pe.wait_ge(turn_emptied, l * NTURN + 7)
                pe.wait_ge(o_emptied, BASE + l * 11 + done)
                if g < 4:
                    for h in range(2):
                        for kt in range(2):
                            last = PE.matmul(O_BANK[64 * h:64 * h + 64, 0:SEQ], v_mla[:, kt, 2 * g + h, :], pt[:, 2 * h + kt, :],
                                             start=kt == 0, stop=kt == 1)
                elif g < 8:
                    h = g - 4
                    for t in range(NT):
                        for kt in range(2):
                            last = PE.matmul(O_BANK[:, t * P:t * P + P], pt[:, kt, t * P:t * P + P], v_diff[:, kt, h * P:(h + 1) * P],
                                             start=kt == 0, stop=kt == 1)
                else:
                    head = g - 8
                    o = 64 * (head % 2)
                    vs = slice(head * HD, head * HD + HD)
                    for kt in range(2):
                        PE.matmul(O_BANK[o:o + 64, 0:SEQ], v_dil[:, kt, 0, vs], pt[:, kt, :], start=kt == 0, stop=False, skip_group_check=True)
                    for dg in (1, 2):
                        for t in range(NT):
                            last = PE.matmul(O_BANK[o:o + 64, t * P:t * P + P], v_dil[:, t, dg, vs], pt[:, 1 + dg, t * P:t * P + P],
                                             start=False, stop=dg == 2, skip_group_check=True)
                last.then_inc(o_full, 1)

            with pe.Fori(0, DEPTH) as l:
                for step in STEPS:
                    what = step[0]
                    if what == "turn":
                        turn(l, step[1])
                    elif what == "w":
                        use_piece(l, step[1])
                    elif what == "score":
                        scores(l, step[1])
                    elif what == "pv":
                        products(l, step[1])
                    elif what == "tq":
                        s = step[1]
                        wait_t(l, step)
                        pe.wait_ge(roped, l * NSTAGE + (s + 1))
                        kind = TILES[STAGED[s]][0]
                        st = stage[:, s % SRING, :]
                        if kind in ("uq", "ukv"):
                            for h in range(4):
                                last = PE.transpose(T_BANK[0:QK_M, h * P:(h + 1) * P], st[:, h * QK_M:(h + 1) * QK_M], ident[:])
                        else:
                            for h in range(4 if kind == "diff" else 3):
                                last = PE.transpose(T_BANK[:, h * P:(h + 1) * P], st[:, h * P:(h + 1) * P], ident[:])
                        last.then_inc(t_full, 1)
                    elif what == "tp":
                        i = step[1]
                        wait_t(l, step)
                        pe.wait_ge(probs_ready, l * 28 + (i + 1))
                        for b in range(4):
                            last = PE.transpose(T_BANK[:, b * P:(b + 1) * P], probs[:, i % 2, b * P:(b + 1) * P], ident[:])
                        last.then_inc(t_full, 1)
                    elif what == "td":
                        t = step[1]
                        wait_t(l, step)
                        pe.wait_ge(diff_rows, l * 2 + (t + 1))
                        for h in range(4):
                            last = PE.transpose(T_BANK[:, h * P:(h + 1) * P], diff_o[:, t, h * P:(h + 1) * P], ident[:])
                        last.then_inc(t_full, 1)


def first_of(n):
    kind, c = PIECES[n][0:2]
    while n not in FIRST_TILE or PIECES[n][0:2] != (kind, c):
        n -= 1
    return FIRST_TILE[n]


def tiles_of(n):
    return 4 if PIECES[n][4] == 1024 else 2


_INS = ['x', 'positions', 'attn_pre_norm', 'w_in', 'mla_q_norm', 'mla_w_uq', 'mla_kv_norm', 'mla_w_ukv', 'diff_lambda',
        'diff_subln', 'w_branch_mla', 'w_branch_dil', 'w_branch_diff', 'w_out', 'attn_post_norm', 'ffn_pre_norm', 'w_up',
        'ffn_conv', 'w_down', 'ffn_post_norm']


def kernel(**inputs):
    import concourse.bacc as _bacc
    from concourse.bass_utils import run_bass_kernel_spmd as _run

    nc = _bacc.Bacc("TRN2", target_bir_lowering=False, num_devices=1)
    arrays, args = {}, {}
    for name in _INS:
        v = np.ascontiguousarray(inputs[name])
        arrays[f"in_{name}_dram"] = v
        args[name] = nc.dram_tensor(f"in_{name}_dram", v.shape, mybir.dt.from_np(v.dtype), kind="ExternalInput").ap()
    out = nc.dram_tensor("out_dram", (1, SEQ, D), F32, kind="ExternalOutput").ap()
    build_trunk(nc, args, out)
    r = _run(nc, [arrays], core_ids=[0])
    return r.results[0]["out_dram"]
```

```python
from contextlib import ExitStack
import math

import numpy as np

import concourse.bass as bass
from concourse import mybir

F32 = mybir.dt.float32
F32R = mybir.dt.float32r
BF16 = mybir.dt.bfloat16
I32 = mybir.dt.int32
ALU = mybir.AluOpType
ACT = mybir.ActivationFunctionType
AX = mybir.AxisListType

P = 128
D = 1024
SEQ = 256
DEPTH = 2
NT = SEQ // P
KD = D // P
EPS = 1e-6

MLA_H, NOPE, ROPE, MLA_V = 8, 64, 32, 64
QK_M = NOPE + ROPE
Q_RANK, KV_RANK = 384, 256
MLA_COLS = Q_RANK + KV_RANK + ROPE
HD = 64
DIL_G, DIL_H = 3, 6
D_FF = 2816
FT = D_FF // P
MLA0 = 3 * D
DIL0 = MLA0 + MLA_COLS
DIFF0 = DIL0 + DIL_G * 3 * DIL_H * HD
MLA_SCALE = float(QK_M) ** -0.5
SCALE = float(HD) ** -0.5
MASKED = -(2.0 ** 100)

NB = 4
X_START = 4
BASE = 1
WAITS = {"attn": (4, 14, 22), "ffn": (12, 24, 6)}
WARM_UP = 60
RING = 3
NU = D_FF // 256


def plan_pieces():
    pieces = []
    for c in range(2):
        pieces += [("mla", c, k, 4, 336) for k in (0, 4)]
    pieces += [("diff", 0, k, 4, 512) for k in (0, 4)]
    pieces += [("diff", 1, 0, 4, 512), ("uq", 0, 0, 3, 384), ("diff", 1, 4, 4, 512), ("uq", 1, 0, 3, 384)]
    pieces += [("diff", 2, 0, 4, 512), ("ukv", 0, 0, 2, 512), ("diff", 2, 4, 4, 512), ("ukv", 1, 0, 2, 512)]
    for c in range(9):
        pieces += [("dil", c, k, 4, 384) for k in (0, 4)]
    for c in range(6):
        pieces += [("gate", c, k, 4, 512) for k in (0, 4)]
    pieces += [("bmla", 0, 0, 2, 1024), ("bmla", 0, 2, 2, 1024)]
    pieces += [("bdiff", 0, 0, 2, 1024), ("bdiff", 0, 2, 2, 1024)]
    pieces += [("bdil", 0, 0, 2, 1024), ("bdil", 0, 2, 1, 1024)]
    for c in range(2):
        pieces += [("out", c, k, 4, 512) for k in (0, 4)]
    for u in range(NU + 1):
        if u < NU:
            pieces += [("up", 2 * u, 0, 8, 256), ("up", 2 * u + 1, 0, 8, 256)]
        if u > 0:
            pieces += [("down", u - 1, 0, 2, 1024)]
    return pieces


PIECES = plan_pieces()
NPIECE = len(PIECES)
OUT0 = PIECES.index(("out", 0, 0, 4, 512))
UP0 = PIECES.index(("up", 0, 0, 8, 256))
JOINED = [PIECES.index(("bdil", 0, 0, 2, 1024)), PIECES.index(("out", 1, 0, 4, 512))]
assert NPIECE % RING == 0
K_TOTAL = {"mla": 8, "diff": 8, "uq": 3, "ukv": 2, "dil": 8, "gate": 8, "bmla": 4, "bdiff": 4, "bdil": 3, "out": 8}


def staged_by(n):
    kind, c, k0, nk, _ = PIECES[n]
    if kind in ("uq", "ukv") or (k0 + nk == 8 and ((kind == "diff" and c < 2) or (kind == "dil" and c % 3 < 2))):
        return 2
    return 0


def plan_steps():
    s = [("turn", "attn"), ("pre",)]
    n = staged = 0
    waiting = []

    def w():
        nonlocal n, staged
        s.append(("w", n))
        for _ in range(staged_by(n)):
            waiting.append((staged, n))
            staged += 1
        n += 1

    def turn_staged(most):
        while waiting and most and waiting[0][1] <= n - 2:
            s.append(("tq", waiting.pop(0)[0]))
            most -= 1

    for _ in range(4):
        w()
    s.append(("latent",))
    w(), w()
    s.append(("turn", "latent"))
    for _ in range(8):
        turn_staged(2)
        w()
    for i in range(28):
        s.append(("score", i))
        if i >= 3 and i % 2 == 1:
            s.append(("pv", (i - 2) // 2))
        for _ in range(4 if i == 15 else 1):
            turn_staged(1)
            if i in (21, 22):
                s.append(("td", i - 21))
            w()
        if i == 19:
            s.append(("heads",))
        if i >= 1 and i - 1 not in (8, 10, 12, 14):
            s.append(("tp", i - 1))
    assert not waiting
    w()
    s.append(("tp", 27))
    w()
    s.append(("pv", 13))
    while n < PIECES.index(("out", 0, 0, 4, 512)):
        w()
    s.append(("turn", "merged"))
    for _ in range(4):
        w()
    s += [("mid",), ("turn", "ffn")]
    while n < NPIECE:
        w()
    s.append(("end",))
    return s


STEPS = plan_steps()

T_ORDER = [x for x in STEPS if x[0] in ("tq", "tp", "td")]
T_OF = {x: n for n, x in enumerate(T_ORDER)}
NTB = len(T_ORDER)
N_EARLY = 10
assert all(x[0] == "tq" for x in T_ORDER[:N_EARLY])


def plan_tiles():
    tiles, first = [], {}
    for n, (kind, c, k0, nk, cols) in enumerate(PIECES):
        if kind == "up" or (kind == "down" and c > 0):
            continue
        if k0:
            continue
        first[n] = len(tiles)
        halves = max(1, cols // 512) if cols == 1024 else 1
        order = [(h, t) for t in range(NT) for h in range(halves)] if kind == "down" else [(h, t) for h in range(halves) for t in range(NT)]
        tiles += [(kind, c, h, t) for h, t in order]
    return tiles, first


TILES, FIRST_TILE = plan_tiles()
NTILE = len(TILES)
assert NTILE % NB == 0
BY_DVE = ("bmla", "bdiff", "bdil", "out", "down")


GROUP_END = {}
for _n, _p in enumerate(PIECES):
    if _p[0] == "up" or (_p[0] == "down" and _p[1] < NU - 1):
        continue
    if _p[0] == "down" or _p[2] + _p[3] == K_TOTAL[_p[0]]:
        _m = max(m for m, x in enumerate(TILES) if x[0] == _p[0] and (_p[0] == "down" or x[1] == _p[1]))
        GROUP_END[_m] = _n
NFULL = NTILE - len(GROUP_END)


def completing_piece(m):
    kind, c = TILES[m][0:2]
    return max(n for n, x in enumerate(PIECES) if x[0] == kind and (kind == "down" or x[1] == c))


DONE_ORDER = sorted(range(NTILE), key=lambda m: (completing_piece(m), m))


def full_count(m):
    return sum(1 for x in DONE_ORDER[:DONE_ORDER.index(m) + 1] if x not in GROUP_END)


def emptied(n):
    who = "dve" if TILES[n][0] in BY_DVE else "act"
    if TILES[n][0] in ("out", "down"):
        while n + 1 < NTILE and TILES[n + 1][0] == TILES[n][0]:
            n += 1
    return who, sum(1 for m in DONE_ORDER[:DONE_ORDER.index(n) + 1] if (TILES[m][0] in BY_DVE) == (who == "dve"))


N_DVE = sum(1 for x in TILES if x[0] in BY_DVE)
N_ACT = NTILE - N_DVE

STAGED = [n for n, (kind, c, h, t) in ((n, TILES[n]) for n in DONE_ORDER)
          if kind in ("uq", "ukv") or (kind == "diff" and c < 2) or (kind == "dil" and c % 3 < 2)]
STAGE_OF = {n: s for s, n in enumerate(STAGED)}
NSTAGE = len(STAGED)
SRING = 4

TURN_BANKS = {"attn": [(0, 2), (2, 2), (4, 2), (6, 2)], "merged": [(0, 2), (2, 2), (4, 2), (6, 2)],
              "ffn": [(0, 2), (2, 2), (4, 2), (6, 2)], "latent": [(0, 2), (2, 2), (4, 1)]}
TURN_BEFORE = {"attn": 0, "latent": 4, "merged": 7, "ffn": 11}
NTURN = 15

NPAR = 3 * FT * 2 + 22 + 1
PRE_A, PRE_F, G_Q, G_KV, G_SUB, LAM = 132, 140, 148, 151, 153, 154


def pieces_2pi():
    out, rest = [], 2 * math.pi
    for _ in range(3):
        e = math.floor(math.log2(rest))
        q = 2.0 ** (e - 7)
        c = math.floor(rest / q) * q
        out.append(c)
        rest -= c
    return out + [float(np.float32(rest))]


def lambda_init(layer):
    return 0.8 - 0.6 * math.exp(-0.3 * layer)


def build_trunk(nc, a, out):
    with ExitStack() as ctx:
        def sb(name, shape, dt=F32, scope=ctx):
            return scope.enter_context(nc.sbuf_tensor(name, shape, dt))

        def sem(name):
            return ctx.enter_context(nc.semaphore(name))

        x = sb("x_rows", [P, NT, D])
        hT_hi = sb("hT_hi", [P, KD, SEQ], F32R)
        hT_lo = sb("hT_lo", [P, KD, SEQ], F32R)
        raw = sb("w_raw", [P, RING, 2048])
        w_hi = sb("w_hi", [P, RING, 2048], F32R)
        w_lo = sb("w_lo", [P, RING, 2048], F32R)
        post_gain = sb("post_gain", [P, D])
        ident = sb("ident", [P, P])
        ident_b = sb("ident_b", [P, P], BF16)
        mask = sb("mask", [P, NT, 512], BF16)
        cosT = sb("cosT", [P, NT, 16])
        sinT = sb("sinT", [P, NT, 16])
        par_all = sb("par_all", [P, DEPTH, NPAR])
        par = sb("par", [P, NPAR])
        small = sb("small", [P, 64])
        rope_a = sb("rope_a", [P, 256])
        rope_b = sb("rope_b", [P, 256])
        minus_half = sb("minus_half", [P, 1])
        half = sb("half", [P, 1])
        head_squares = sb("head_squares", [P, SEQ])
        mean_squares = sb("mean_squares", [P, 6])
        roots = sb("roots", [P, 6])

        with ExitStack() as one:
            diff_qT = sb("diff_qT", [P, 4, SEQ], scope=one)
            diff_kT = sb("diff_kT", [P, 4, SEQ], scope=one)
            mla_qT = sb("mla_qT", [P, MLA_H, SEQ], scope=one)
            mla_kT = sb("mla_kT", [P, MLA_H, SEQ], scope=one)
            mla_seq = sb("mla_seq", [P, NT, 704], scope=one)
            v_mla = sb("v_mla", [P, NT, MLA_H, MLA_V], scope=one)
            v_diff = sb("v_diff", [P, NT, 512], scope=one)
            sb("pad_gates", [P, 640], scope=one)
            dil_qT = sb("dil_qT", [P, 3, DIL_G, SEQ], scope=one)
            dil_kT = sb("dil_kT", [P, 3, DIL_G, SEQ], scope=one)
            v_dil = sb("v_dil", [P, NT, DIL_G, 384], scope=one)
            stage = sb("stage", [P, SRING, 512], scope=one)
            probs = sb("probs", [P, 2, 512], scope=one)
            probsT = sb("probsT", [P, 2, 4, SEQ], scope=one)
            diff_o = sb("diff_o", [P, NT, 512], scope=one)
        with ExitStack() as two:
            diff_oT = sb("diff_oT", [P, 2, 4, SEQ], F32R, scope=two)
            mla_oT = sb("mla_oT", [P, 4, 2, SEQ], F32R, scope=two)
            gates = sb("gates", [P, NT, 3 * D], scope=two)
            dil_oT = sb("dil_oT", [P, 3, 3, SEQ], F32R, scope=two)
            merged = sb("merged", [P, NT, D], scope=two)
            sb("pad_merged", [P, 256], scope=two)
            sb("pad_two", [P, NT * DIL_G * 384 + SRING * 512], scope=two)
            xn = sb("x_normed", [P, NT, D], scope=two)
        with ExitStack() as three:
            sb("pad_three", [P, 2 * 4 * SEQ + 4 * 2 * SEQ + NT * 3 * D], scope=three)
            latT_hi = sb("latT_hi", [P, 5, SEQ], F32R, scope=three)
            latT_lo = sb("latT_lo", [P, 5, SEQ], F32R, scope=three)
            sb("pad_three_b", [P, 2048 - 512], scope=three)
        with ExitStack() as four:
            conv = sb("conv_out", [P, 2, 2, 512], scope=four)
            g_hi = sb("g_hi", [P, 2, 512], F32R, scope=four)
            g_lo = sb("g_lo", [P, 2, 512], F32R, scope=four)
            square_ffn = sb("square_ffn", [P, D], scope=four)
            par_rows = sb("par_rows", [44, 4 * DEPTH, P], scope=four)
            lam_rows = sb("lam_rows", [P, DEPTH, 4, HD], scope=four)
            pos_i = sb("pos_i", [P, NT], I32, scope=four)
            pos_f = sb("pos_f", [P, NT], scope=four)
            ang = sb("ang", [P, NT, 16], scope=four)
            turns = sb("turns", [P, NT, 16], scope=four)
            inv_freq = sb("inv_freq", [P, 16], scope=four)
            lam_prod = sb("lam_prod", [P, DEPTH, 2, HD], scope=four)
            lam_sum = sb("lam_sum", [P, DEPTH, 2], scope=four)
            lam_exp = sb("lam_exp", [P, DEPTH, 2], scope=four)

        bank = [ctx.enter_context(nc.psum_tensor(f"bank{i}", [P, 512], F32)) for i in range(8)]
        S_BANK, O_BANK = (bank[4], bank[5]), bank[7]

        def t_bank(n):
            return bank[6 + n % 2] if n < N_EARLY else bank[6]

        ss = small[:, 0:8]
        inverse_roots = small[:, 8:16]
        mean_eps = small[:, 32:40]
        negmax = small[:, 40:44]
        rowsum = small[:, 44:48]
        rinv = small[:, 48:52]
        rstd_attn = small[:, 52:54]
        half_rstd = small[:, 54:56]
        distance = rope_a[:, 0:P].bitcast(I32)
        other_class = rope_b[:, 0:P]

        raw_landed = [sem(f"raw_landed{i}") for i in range(RING)]
        hi_done, lo_done, piece_used = sem("hi_done"), sem("lo_done"), sem("piece_used")
        tile_full, tile_emptied_act, tile_emptied_dve = sem("tile_full"), sem("tile_emptied_act"), sem("tile_emptied_dve")
        roped = sem("roped")
        turn_full, turn_hi, turn_emptied = sem("turn_full"), sem("turn_hi"), sem("turn_emptied")
        t_full, t_emptied = sem("t_full"), sem("t_emptied")
        score_full, max_done, exp_done, probs_ready = sem("score_full"), sem("max_done"), sem("exp_done"), sem("probs_ready")
        o_full, o_hi, o_emptied = sem("o_full"), sem("o_hi"), sem("o_emptied")
        diff_rows, diff_hi, diff_lo = sem("diff_rows"), sem("diff_hi"), sem("diff_lo")
        squares, rstd_done = sem("squares"), sem("rstd_done")
        ffn_squares, xn_done = sem("ffn_squares"), sem("xn_done")
        lat_squares, lat_normed = sem("lat_squares"), sem("lat_normed")
        attn_means, latent_means, latent_roots = sem("attn_means"), sem("latent_means"), sem("latent_roots")
        head_means, head_roots = sem("head_means"), sem("head_roots")
        means_ready, roots_ready = sem("means_ready"), sem("roots_ready")
        merged_ready = sem("merged_ready")
        post_squares, x_ready = sem("post_squares"), sem("x_ready")
        conv_mid, conv_done = sem("conv_mid"), sem("conv_done")
        gelu_done, g_ready, g_hi_done, g_lo_done = sem("gelu_done"), sem("g_ready"), sem("g_hi_done"), sem("g_lo_done")
        gain_landed = sem("gain_landed")
        x_landed = sem("x_landed")
        positions_landed, parameters_landed, par_turned = sem("positions_landed"), sem("parameters_landed"), sem("par_turned")
        lambda_landed = sem("lambda_landed")
        ident_ready, distance_ready, class_ready, masks_ready = sem("ident_ready"), sem("distance_ready"), sem("class_ready"), sem("masks_ready")
        angles, tables, lam_sums, lam_exps = sem("angles"), sem("tables"), sem("lam_sums"), sem("lam_exps")
        par_ready, out_landed = sem("par_ready"), sem("out_landed")
        slot_claimed, key_claimed = sem("slot_claimed"), sem("key_claimed")

        GAINS = (("attn_pre_norm", 0, 8), ("ffn_pre_norm", 8, 8), ("mla_q_norm", 16, 3), ("mla_kv_norm", 19, 2), ("diff_subln", 21, 1))
        N_PARAMETERS = len(GAINS) + 1

        def weight_source(l, kind, c, k0, nk, cols):
            if kind in ("mla", "diff", "dil", "gate"):
                c0 = {"mla": MLA0 + 336 * c, "diff": DIFF0 + 512 * c, "dil": DIL0 + 384 * c, "gate": 512 * c}[kind]
                src = a["w_in"]
            elif kind == "uq":
                src, c0 = a["mla_w_uq"], 384 * c
            elif kind == "ukv":
                src, c0 = a["mla_w_ukv"], 512 * c
            elif kind in ("bmla", "bdil", "bdiff"):
                src, c0 = a["w_branch_" + kind[1:]], 0
            elif kind == "out":
                src, c0 = a["w_out"], 512 * c
            elif kind == "up":
                src, c0 = a["w_up"], (c % 2) * D_FF + 256 * (c // 2)
            else:
                src, c0, k0 = a["w_down"], 0, 2 * c
            view = src.rearrange("l (k p) n -> l p k n", p=P)
            return view[l, :, k0:k0 + nk, c0:c0 + cols]

        def cut(buf, n):
            nk, cols = PIECES[n][3:5]
            return buf[:, n % RING, 0:nk * cols].rearrange("p (k n) -> p k n", k=nk)

        def own_order(cols):
            return cols.rearrange("p (j r) -> p r j", r=4)

        def by_class(cols):
            return cols.rearrange("p (r j) -> p r j", r=4)

        def own_order2(cols):
            return cols.rearrange("p (c j r) -> p c r j", c=2, r=4)

        def by_class2(cols):
            return cols.rearrange("p (c r j) -> p c r j", c=2, r=4)

        def class_rows(dram):
            view = dram[0].rearrange("(j r) d -> r j d", r=4)
            return [(slice(64 * (r % 2), 64 * (r % 2) + 64), r // 2, view[r]) for r in range(4)]

        def wait_tile(eng, l, m):
            if m in GROUP_END:
                eng.wait_ge(piece_used, l * NPIECE + (RING + GROUP_END[m] + 1))
            else:
                eng.wait_ge(tile_full, l * NFULL + full_count(m))

        block = ctx.enter_context(nc.Block())

        @block.sync
        def _(sp):
            for name, r0, rows in GAINS:
                sp.dma_start(par_rows[r0:r0 + rows, 3 * DEPTH:4 * DEPTH, :],
                             a[name].rearrange("l (c p) -> c l p", p=P)).then_inc(parameters_landed, 16)
            sp.dma_start(par_rows[:, 0:3 * DEPTH, :], a["ffn_conv"].rearrange("l t (c p) -> c (l t) p", p=P)).then_inc(parameters_landed, 16)
            with sp.Fori(0, DEPTH) as l:
                for n, piece in enumerate(PIECES):
                    sp.wait_ge(lo_done, l * NPIECE + (n + 1))
                    sp.sem_inc(slot_claimed, 1)
                    sp.dma_start(cut(raw, n), weight_source(l, *piece)).then_inc(raw_landed[n % RING], 16)
            for part, t, dst in class_rows(out):
                sp.wait_ge(x_ready, X_START + 8 * DEPTH - 2 * (NT - 1 - t))
                sp.dma_start(dst, x[part, t, :]).then_inc(out_landed, 16)
            sp.wait_ge(out_landed, 16 * 4)

        @block.gpsimd
        def _(pool):
            nc.gpsimd.memset(ident[:], 0.0)
            nc.gpsimd.memset(minus_half[:], -0.5)
            nc.gpsimd.memset(half[:], 0.5)
            pool.drain()
            nc.gpsimd.affine_select(out=ident[:], in_=ident[:], compare_op=ALU.not_equal, fill=1.0, base=0,
                                    pattern=[[-1, P]], channel_multiplier=1)
            pool.drain().then_inc(ident_ready, 1)
            pool.dma_start(lam_rows[:, :, :, :].rearrange("p l v d -> p (l v d)"),
                           a["diff_lambda"].rearrange("l v d -> (l v d)").partition_broadcast(P)).then_inc(lambda_landed, 16)
            positions = a["positions"][0, :].rearrange("(j t h) -> h j t", t=NT, h=2)
            for h in range(2):
                pool.dma_start(pos_i[64 * h:64 * h + 64, :], positions[h], allow_slow_non_contiguous=True).then_inc(positions_landed, 16)
            nc.gpsimd.iota(distance, pattern=[[-1, P]], base=P, channel_multiplier=1)
            pool.drain().then_inc(distance_ready, 1)
            nc.gpsimd.memset(ident_b[:], 0.0)
            nc.gpsimd.memset(mask[:], 0.0)
            pool.drain()
            nc.gpsimd.affine_select(out=ident_b[:], in_=ident_b[:], compare_op=ALU.not_equal, fill=1.0, base=0,
                                    pattern=[[-1, P]], channel_multiplier=1)
            for t in range(NT):
                for h in range(2):
                    rq = 2 * t + h
                    m = mask[64 * h:64 * h + 64, t, 0:SEQ].rearrange("p (r j) -> p r j", r=4)
                    nc.gpsimd.affine_select(out=m, in_=m, compare_op=ALU.is_ge, fill=MASKED, base=rq + 64,
                                            pattern=[[-1, 4], [-4, 64]], channel_multiplier=4)
                    pool.drain()
                    nc.gpsimd.affine_select(out=m, in_=m, compare_op=ALU.is_ge, fill=MASKED, base=64 - rq,
                                            pattern=[[1, 4], [4, 64]], channel_multiplier=-4)
                    pool.drain()
            for t in range(NT):
                for g in range(2):
                    c0 = SEQ + P * g
                    nc.gpsimd.memset(mask[0:64, t, c0 + 64:c0 + 128], MASKED)
                    pool.drain()
                    nc.gpsimd.memset(mask[64:128, t, c0:c0 + 64], MASKED)
                    pool.drain()
            pool.wait_ge(class_ready, 1)
            for t in range(NT):
                nc.gpsimd.tensor_tensor(mask[:, t, 384:512], mask[:, t, 384:512], other_class, ALU.add)
            pool.drain().then_inc(masks_ready, 1)

            def rope(view, heads, first, half, t):
                step = 16 // half
                xr = view[:, :, first:first + 2 * half].rearrange("p h (s f) -> p h s f", s=2)
                shape = [P, heads, 2, half]
                c = cosT[:, t, ::step].rearrange("p (a b f) -> p a b f", a=1, b=1).broadcast_to(shape)
                s = sinT[:, t, ::step].rearrange("p (a b f) -> p a b f", a=1, b=1).broadcast_to(shape)
                n = heads * 2 * half
                ca = rope_a[:, 0:n].rearrange("p (h s f) -> p h s f", h=heads, s=2)
                sa = rope_b[:, 0:n].rearrange("p (h s f) -> p h s f", h=heads, s=2)
                nc.gpsimd.tensor_tensor(ca, xr, c, ALU.mult)
                nc.gpsimd.tensor_tensor(sa, xr, s, ALU.mult)
                pool.drain()
                nc.gpsimd.tensor_tensor(xr[:, :, 0, :], ca[:, :, 0, :], sa[:, :, 1, :], ALU.subtract)
                return nc.gpsimd.tensor_tensor(xr[:, :, 1, :], ca[:, :, 1, :], sa[:, :, 0, :], ALU.add)

            pool.wait_ge(tables, 1)
            with pool.Fori(0, DEPTH) as l:
                pool.wait_ge(attn_means, l + 1)
                nc.gpsimd.tensor_tensor(rstd_attn, mean_eps[:, 0:2], minus_half[:].broadcast_to([P, 2]), ALU.pow)
                pool.drain()
                nc.gpsimd.tensor_tensor(half_rstd, rstd_attn, half[:].broadcast_to([P, 2]), ALU.mult).then_inc(rstd_done, 1)
                for n in DONE_ORDER:
                    kind, c, _, t = TILES[n]
                    if kind == "mla" and c == 1:
                        pool.drain()
                        pool.wait_ge(tile_emptied_act, l * N_ACT + emptied(n)[1])
                        rope(mla_seq[:, t:t + 1, 640:672], 1, 0, 16, t)
                        if t == NT - 1:
                            pool.drain()
                            pool.wait_ge(latent_means, l + 1)
                            nc.gpsimd.tensor_tensor(inverse_roots[:, 0:4], mean_eps[:, 0:4], minus_half[:].broadcast_to([P, 4]), ALU.pow).then_inc(latent_roots, 1)
                    if n not in STAGE_OF:
                        continue
                    pool.drain()
                    st = stage[:, STAGE_OF[n] % SRING, :]
                    pool.wait_ge(tile_emptied_act, l * N_ACT + emptied(n)[1])
                    if kind == "uq":
                        rope(st[:, 0:384].rearrange("p (h w) -> p h w", h=4), 4, NOPE, 16, t).then_inc(roped, 1)
                    elif kind == "ukv":
                        pool.sem_inc(key_claimed, 1)
                        kr = mla_seq[:, t:t + 1, 640:672].broadcast_to([P, 4, ROPE])
                        nc.gpsimd.tensor_copy(st[:, 0:384].rearrange("p (h w) -> p h w", h=4)[:, :, NOPE:QK_M], kr).then_inc(roped, 1)
                    elif kind == "diff":
                        rope(st.rearrange("p (h w) -> p h w", h=8), 8, 0, 8, t).then_inc(roped, 1)
                    else:
                        rope(st[:, 0:384].rearrange("p (h w) -> p h w", h=6), 6, 0, 8, t).then_inc(roped, 1)
                pool.wait_ge(head_means, l + 1)
                nc.gpsimd.tensor_tensor(inverse_roots[:, 0:8], mean_eps[:, 0:8], minus_half[:].broadcast_to([P, 8]), ALU.pow).then_inc(head_roots, 1)
                for j in range(6):
                    pool.wait_ge(means_ready, l * 6 + (j + 1))
                    nc.gpsimd.tensor_tensor(roots[:, j:j + 1], mean_squares[:, j:j + 1], minus_half[:], ALU.pow).then_inc(roots_ready, 1)

        @block.scalar
        def _(act):
            act.sem_inc(t_emptied, BASE)
            tokens = a["x"][0].rearrange("(j t h) d -> h j t d", t=NT, h=2)
            for h in range(2):
                act.dma_start(x[64 * h:64 * h + 64, :, :], tokens[h]).then_inc(x_landed, 16)
            act.wait_ge(lam_sums, 1)
            nc.scalar.activation(lam_exp[:], lam_sum[:], ACT.Exp).then_inc(lam_exps, 1)
            act.wait_ge(angles, 1)
            nc.scalar.activation(sinT[:], ang[:], ACT.Sin)
            nc.scalar.activation(cosT[:], turns[:], ACT.Sin).then_inc(tables, 1)

            def split_hi(l, n):
                nk, cols = PIECES[n][3:5]
                act.wait_ge(raw_landed[n % RING], (l * (NPIECE // RING) + (n // RING + 1)) * 16)
                act.wait_ge(piece_used, l * NPIECE + (n + 1))
                nc.scalar.activation(w_hi[:, n % RING, 0:nk * cols], raw[:, n % RING, 0:nk * cols], ACT.Copy).then_inc(hi_done, 1)

            def empty_tile(l, n):
                kind, c, h, t = TILES[n]
                rstd = rstd_attn[:, t:t + 1]
                if n == 0:
                    act.wait_ge(rstd_done, l + 1)
                src = bank[n % NB]
                wait_tile(act, l, n)
                if n in STAGE_OF:
                    s = STAGE_OF[n]
                    if s >= SRING:
                        act.wait_ge(t_full, l * NTB + (T_OF[("tq", s - SRING)] + 1))
                    dst = stage[:, s % SRING, :]
                    if kind == "uq":
                        last = nc.scalar.activation(dst[:, 0:384], src[:, 0:384], ACT.Copy)
                    elif kind == "dil":
                        last = nc.scalar.activation(dst[:, 0:384], src[:, 0:384], ACT.Copy, scale=rstd)
                    elif kind == "diff":
                        last = nc.scalar.activation(dst, src[:], ACT.Copy, scale=rstd)
                    else:
                        kv = src[:].rearrange("p (h w) -> p h w", h=4)
                        nc.scalar.activation(dst[:, 0:384].rearrange("p (h w) -> p h w", h=4)[:, :, 0:NOPE], kv[:, :, 0:NOPE], ACT.Copy)
                        last = nc.scalar.activation(v_mla[:, t, 4 * c:4 * c + 4, :], kv[:, :, NOPE:], ACT.Copy)
                elif kind == "mla":
                    last = nc.scalar.activation(mla_seq[:, t, 336 * c:336 * c + 336], src[:, 0:336], ACT.Copy, scale=rstd)
                elif kind == "diff":
                    last = nc.scalar.activation(v_diff[:, t, :], src[:], ACT.Copy, scale=rstd)
                elif kind == "dil":
                    last = nc.scalar.activation(v_dil[:, t, c // 3, :], src[:, 0:384], ACT.Copy, scale=rstd)
                else:
                    last = nc.scalar.activation(gates[:, t, 512 * c:512 * c + 512], src[:], ACT.Tanh, scale=half_rstd[:, t:t + 1])
                last.then_inc(tile_emptied_act, 1)

            def empty_t(l, key):
                n = T_OF[key]
                T_BANK = t_bank(n)
                what, i = key
                act.wait_ge(t_full, l * NTB + (n + 1))
                if what == "tq":
                    kind, c, h, t = TILES[STAGED[i]]
                    rows = slice(t * P, (t + 1) * P)
                    if kind == "uq" or kind == "ukv":
                        dst = (mla_qT if kind == "uq" else mla_kT)[0:QK_M, 4 * c:4 * c + 4, rows]
                        nc.scalar.activation(dst, T_BANK[0:QK_M, :].rearrange("p (h q) -> p h q", h=4), ACT.Copy,
                                             scale=MLA_SCALE if kind == "uq" else 1.0).then_inc(t_emptied, 1)
                    elif kind == "diff":
                        dst = (diff_qT if c == 0 else diff_kT)[:, :, rows]
                        nc.scalar.activation(dst, T_BANK[:].rearrange("p (h q) -> p h q", h=4), ACT.Copy,
                                             scale=SCALE if c == 0 else 1.0).then_inc(t_emptied, 1)
                    else:
                        dst = (dil_qT if c % 3 == 0 else dil_kT)[:, :, c // 3, rows]
                        nc.scalar.activation(dst, T_BANK[:, 0:384].rearrange("p (h q) -> p h q", h=3), ACT.Copy,
                                             scale=SCALE if c % 3 == 0 else 1.0).then_inc(t_emptied, 1)
                elif what == "tp":
                    g, qt = i // 2, i % 2
                    if g >= 2:
                        act.wait_ge(o_full, l * 14 + (g - 1))
                    if 8 <= i < 16:
                        nc.scalar.activation(probsT[:, g % 2, 0:2, :].rearrange("p k (t q) -> p t k q", t=2),
                                             T_BANK[:].rearrange("p (t k q) -> p t k q", t=2, k=2), ACT.Copy).then_inc(t_emptied, 1)
                    else:
                        nc.scalar.activation(probsT[:, g % 2, :, qt * P:qt * P + P], T_BANK[:].rearrange("p (b q) -> p b q", b=4),
                                             ACT.Copy).then_inc(t_emptied, 1)
                else:
                    nc.scalar.activation(diff_o[:, i, :], T_BANK[:], ACT.Copy, scale=par[:, G_SUB:G_SUB + 1]).then_inc(t_emptied, 1)
                    act.wait_ge(t_emptied, BASE + l * NTB + (n + 1))
                    nc.scalar.activation(diff_oT[:, 0, :, i * P:i * P + P], diff_o[:, i, :].rearrange("p (h q) -> p h q", h=4),
                                         ACT.Copy).then_inc(diff_hi, 1)

            def empty_turn(l, what):
                if what == "attn":
                    act.wait_ge(par_ready, l + 1)
                for b, (k0, nk) in enumerate(TURN_BANKS[what]):
                    m = TURN_BEFORE[what] + b
                    act.wait_ge(turn_full, l * NTURN + (m + 1))
                    src = bank[4 + b]
                    if what == "merged":
                        last = nc.scalar.activation(hT_hi[:, k0:k0 + 2, :], src[:].rearrange("p (k q) -> p k q", k=2), ACT.Copy, scale=0.5)
                    else:
                        dst = latT_hi if what == "latent" else hT_hi
                        g0 = {"attn": PRE_A, "ffn": PRE_F, "latent": G_Q}[what]
                        for k in range(nk):
                            col, from_bank = dst[:, k0 + k, :], src[:, k * SEQ:(k + 1) * SEQ]
                            if what == "ffn":
                                col, from_bank = own_order(col), by_class(from_bank)
                            last = nc.scalar.activation(col, from_bank, ACT.Copy,
                                                        scale=par[:, g0 + k0 + k:g0 + k0 + k + 1])
                    last.then_inc(turn_hi, 1)

            def pre_attn(l):
                act.wait_ge(x_landed, 16 * 2)
                act.wait_ge(x_ready, X_START + l * 8)
                act.dma_start(post_gain[:], a["attn_post_norm"][l, :].partition_broadcast(P)).then_inc(gain_landed, 16)
                for t in range(NT):
                    last = nc.scalar.activation(xn[:, t, :], x[:, t, :], ACT.Square, scale=1.0 / 32, accum_out=ss[:, 2 * t:2 * t + 1])
                last.then_inc(squares, 1)

            def post_square(l, which, t, h):
                wait_tile(act, l, post_tile(which, t, h))
                nc.scalar.activation(xn[:, t, h * 512:h * 512 + 512], bank[post_tile(which, t, h) % NB][:], ACT.Square, scale=1.0 / 32,
                                     accum_out=ss[:, 4 + 2 * t + h:5 + 2 * t + h]).then_inc(post_squares, 1)

            def pre_square(l, t):
                for h in range(2):
                    act.wait_ge(x_ready, l * 8 + (X_START + 2 * t + h + 1))
                    last = nc.scalar.activation(xn[:, t, h * 512:h * 512 + 512], x[:, t, h * 512:h * 512 + 512], ACT.Square, scale=1.0 / 32,
                                                accum_out=ss[:, 2 * t + h:2 * t + h + 1])
                last.then_inc(ffn_squares, 1)

            def pre_scale(l, t):
                act.wait_ge(roots_ready, l * 6 + (ROOT["pre", t] + 1))
                for h in range(2):
                    s = slice(h * 512, h * 512 + 512)
                    nc.scalar.activation(xn[:, t, s], x[:, t, s], ACT.Copy, scale=roots[:, ROOT["pre", t]:ROOT["pre", t] + 1]).then_inc(xn_done, 1)

            with act.Fori(0, DEPTH) as l:
                split_hi(l, 0)
                for step in STEPS:
                    what = step[0]
                    if what == "pre":
                        split_hi(l, 1)
                        pre_attn(l)
                    elif what == "turn":
                        empty_turn(l, step[1])
                        if step[1] == "ffn":
                            split_hi(l, UP0 + 1)
                    elif what == "mid":
                        post_square(l, 0, 0, 1)
                        pre_square(l, 0)
                        post_square(l, 0, 1, 1)
                        pre_scale(l, 0)
                        pre_square(l, 1)
                        act.dma_start(post_gain[:], a["ffn_post_norm"][l, :].partition_broadcast(P)).then_inc(gain_landed, 16)
                        pre_scale(l, 1)
                    elif what == "end":
                        for t in range(NT):
                            for h in range(2):
                                post_square(l, 1, t, h)
                    elif what == "latent":
                        for t in range(NT):
                            act.wait_ge(tile_emptied_act, l * N_ACT + 4)
                            nc.scalar.activation(xn[:, t, 0:Q_RANK], mla_seq[:, t, 0:Q_RANK], ACT.Square,
                                                 accum_out=ss[:, 2 * t:2 * t + 1])
                            nc.scalar.activation(xn[:, t, 512:512 + KV_RANK], mla_seq[:, t, Q_RANK:Q_RANK + KV_RANK], ACT.Square,
                                                 accum_out=ss[:, 2 * t + 1:2 * t + 2]).then_inc(lat_squares, 1)
                    elif what in ("tq", "tp", "td"):
                        empty_t(l, step)
                    elif what == "score":
                        i = step[1]
                        act.wait_ge(max_done, l * 28 + (i + 1))
                        if 10 <= i <= 16 and i % 2 == 0:
                            act.wait_ge(probs_ready, l * 28 + i)
                        elif i >= 2:
                            act.wait_ge(t_full, l * NTB + (T_OF[("tp", i - 2)] + 1))
                        b = i % 2
                        if i < 16:
                            for h in range(2):
                                last = nc.scalar.activation(probs[:, b, h * SEQ:(h + 1) * SEQ], S_BANK[b][:, h * SEQ:(h + 1) * SEQ], ACT.Exp,
                                                            bias=negmax[:, 2 * b + h:2 * b + h + 1],
                                                            accum_out=rowsum[:, 2 * b + h:2 * b + h + 1])
                        else:
                            last = nc.scalar.activation(probs[:, b, :], S_BANK[b][:], ACT.Exp, bias=negmax[:, 2 * b:2 * b + 1],
                                                        accum_out=rowsum[:, 2 * b:2 * b + 1])
                        last.then_inc(exp_done, 1)
                    elif what == "pv":
                        g = step[1]
                        if g < 4 or g >= 8:
                            act.wait_ge(o_full, l * 14 + (g + 1))
                            if g < 4:
                                nc.scalar.activation(mla_oT[:, g, 0, :], O_BANK[:, 0:SEQ], ACT.Copy).then_inc(o_hi, 1)
                            elif g % 2 == 1:
                                nc.scalar.activation(dil_oT[:, (g - 8) // 2, 0, :], O_BANK[:, 0:SEQ], ACT.Copy).then_inc(o_hi, 1)
                    elif what == "w":
                        n = step[1]
                        kind, c, k0, nk, cols = PIECES[n]
                        if n + 2 < NPIECE and n != UP0 - 1:
                            split_hi(l, n + 2)
                        if kind == "out" and c == 0 and k0 == 4:
                            for t in range(NT):
                                post_square(l, 0, t, 0)
                        if kind == "up":
                            u, b = c // 2, c % 2
                            act.wait_ge(piece_used, l * NPIECE + (RING + n + 1))
                            if u >= 2:
                                act.wait_ge(g_lo_done, l * NU + (u - 1))
                            for j in range(2):
                                ch = 22 * b + 2 * u + j
                                last = nc.scalar.activation(conv[:, u % 2, b, j * SEQ:(j + 1) * SEQ],
                                                            bank[4 + c % 4][:, j * SEQ:(j + 1) * SEQ], ACT.Copy,
                                                            scale=par[:, 44 + ch:45 + ch])
                            last.then_inc(conv_mid, 1)
                            if c % 2 == 1:
                                act.wait_ge(conv_done, BASE + l * 2 * NU + c)
                                nc.scalar.activation(conv[:, u % 2, 0, :], conv[:, u % 2, 0, :], ACT.Gelu_apprx_tanh).then_inc(gelu_done, 1)
                                act.wait_ge(g_ready, l * NU + (u + 1))
                                if u >= 2:
                                    act.wait_ge(piece_used, l * NPIECE + (RING + PIECES.index(("down", u - 2, 0, 2, 1024)) + 1))
                                nc.scalar.activation(by_class2(g_hi[:, u % 2, :]), own_order2(conv[:, u % 2, 1, :]), ACT.Copy).then_inc(g_hi_done, 1)
                        elif kind != "down" and k0 + nk == K_TOTAL[kind] and kind not in BY_DVE:
                            f = first_of(n)
                            for m in range(f, f + tiles_of(n)):
                                empty_tile(l, m)

        @block.vector
        def _(dve):
            V = nc.vector

            V.sem_inc(lo_done, RING)
            for started in (tile_emptied_dve, conv_done, o_emptied):
                V.sem_inc(started, BASE)
            V.sem_inc(x_ready, X_START)
            inv = np.power(500000.0, -np.arange(0, ROPE, 2, dtype=np.float64) / ROPE).astype(np.float32)
            for k in range(16):
                V.memset(inv_freq[:, k:k + 1], float(inv[k]))
            dve.wait_ge(lambda_landed, 16)
            V.tensor_tensor(lam_prod[:], lam_rows[:, :, 0:4:2, :], lam_rows[:, :, 1:4:2, :], ALU.mult)
            dve.drain()
            V.tensor_reduce(lam_sum[:], lam_prod[:], AX.X, ALU.add).then_inc(lam_sums, 1)
            dve.wait_ge(positions_landed, 16 * 2)
            V.tensor_copy(pos_f[:], pos_i[:])
            dve.drain()
            shape = [P, NT, 16]
            V.tensor_tensor(ang[:], pos_f[:].rearrange("p (a o) -> p a o", o=1).broadcast_to(shape),
                            inv_freq[:].rearrange("p (o f) -> p o f", o=1).broadcast_to(shape), ALU.mult)
            dve.drain()
            magic = 1.5 * 2.0 ** 23
            V.tensor_scalar(turns[:], ang[:], 1.0 / (2 * math.pi), None, ALU.mult)
            dve.drain()
            V.tensor_scalar(turns[:], turns[:], magic, None, ALU.add)
            dve.drain()
            V.tensor_scalar(turns[:], turns[:], -magic, None, ALU.add)
            dve.drain()
            for part in pieces_2pi():
                V.scalar_tensor_tensor(out=ang[:], in0=turns[:], scalar=-part, in1=ang[:], op0=ALU.mult, op1=ALU.add)
                dve.drain()
            top = float(np.float32(3.1415925))
            V.tensor_scalar(ang[:], ang[:], top, -top, ALU.min, ALU.max)
            dve.drain()
            V.tensor_scalar(turns[:], ang[:], -1.0, None, ALU.mult)
            dve.drain()
            V.tensor_tensor(turns[:], turns[:], ang[:], ALU.min)
            dve.drain()
            V.tensor_scalar(turns[:], turns[:], math.pi / 2, None, ALU.add).then_inc(angles, 1)
            dve.wait_ge(par_turned, 1)
            for l in range(DEPTH):
                V.tensor_copy(par_all[:, l, 0:132], bank[0][:, 132 * l:132 * l + 132])
                V.tensor_copy(par_all[:, l, 132:154], bank[0][:, 264 + 22 * l:264 + 22 * l + 22])
            dve.wait_ge(distance_ready, 1)
            V.tensor_scalar(distance, distance, 3, None, ALU.bitwise_and)
            dve.drain()
            V.tensor_copy(other_class, distance)
            dve.drain()
            V.tensor_scalar(other_class, other_class, 0.0, MASKED, ALU.is_gt, ALU.mult).then_inc(class_ready, 1)
            dve.drain()
            dve.wait_ge(lam_exps, 1)
            for l in range(DEPTH):
                V.tensor_scalar(par_all[:, l, G_SUB:G_SUB + 1], par_all[:, l, G_SUB:G_SUB + 1], 1.0 - lambda_init(l), None, ALU.mult)
                V.tensor_scalar(par_all[:, l, LAM:LAM + 1], lam_exp[:, l, 1:2], lam_exp[:, l, 0:1], -lambda_init(l), ALU.subtract, ALU.add)

            def split_lo(l, n):
                nk, cols = PIECES[n][3:5]
                s = slice(0, nk * cols)
                dve.wait_ge(hi_done, l * NPIECE + (n + 1))
                V.tensor_tensor(w_lo[:, n % RING, s], raw[:, n % RING, s], w_hi[:, n % RING, s].bitcast(F32), ALU.subtract).then_inc(lo_done, 1)

            def empty_turn(l, what):
                for b, (k0, nk) in enumerate(TURN_BANKS[what]):
                    m = TURN_BEFORE[what] + b
                    dve.wait_ge(turn_hi, l * NTURN + (m + 1))
                    src = bank[4 + b]
                    if what == "merged":
                        last = V.scalar_tensor_tensor(out=hT_lo[:, k0:k0 + 2, :], in0=src[:].rearrange("p (k q) -> p k q", k=2), scalar=0.5,
                                                      in1=hT_hi[:, k0:k0 + 2, :].bitcast(F32), op0=ALU.mult, op1=ALU.subtract)
                    else:
                        hi, lo = (latT_hi, latT_lo) if what == "latent" else (hT_hi, hT_lo)
                        g0 = {"attn": PRE_A, "ffn": PRE_F, "latent": G_Q}[what]
                        for k in range(nk):
                            lo_k, hi_k, from_bank = lo[:, k0 + k, :], hi[:, k0 + k, :].bitcast(F32), src[:, k * SEQ:(k + 1) * SEQ]
                            if what == "ffn":
                                lo_k, hi_k, from_bank = own_order(lo_k), own_order(hi_k), by_class(from_bank)
                            last = V.scalar_tensor_tensor(out=lo_k, in0=from_bank, scalar=par[:, g0 + k0 + k:g0 + k0 + k + 1],
                                                          in1=hi_k, op0=ALU.mult, op1=ALU.subtract)
                    last.then_inc(turn_emptied, 1)

            def negmax_of(l, i):
                b = i % 2
                dve.wait_ge(score_full, l * 28 + (i + 1))
                if i < 16:
                    V.tensor_reduce(negmax[:, 2 * b:2 * b + 2], S_BANK[b][:].rearrange("p (h k) -> p h k", h=2), AX.X, ALU.max,
                                    negate=True).then_inc(max_done, 1)
                else:
                    V.tensor_reduce(negmax[:, 2 * b:2 * b + 1], S_BANK[b][:], AX.X, ALU.max, negate=True).then_inc(max_done, 1)

            def normalise(l, i):
                b = i % 2
                dve.wait_ge(exp_done, l * 28 + (i + 1))
                w = 2 if i < 16 else 1
                V.reciprocal(rinv[:, 2 * b:2 * b + w], rowsum[:, 2 * b:2 * b + w])
                dve.drain()
                if i < 8:
                    for h in range(2):
                        s = slice(h * SEQ, (h + 1) * SEQ)
                        last = V.tensor_scalar(probs[:, b, s], probs[:, b, s], rinv[:, 2 * b + h:2 * b + h + 1], None, ALU.mult)
                elif i < 16 and b == 0:
                    for t in range(NT):
                        s = slice(t * SEQ, (t + 1) * SEQ)
                        last = V.tensor_scalar(probs[:, 0, s], probs[:, 0, s], rinv[:, t:t + 1], None, ALU.mult)
                elif i < 16:
                    V.tensor_scalar(rinv[:, 2:4], rinv[:, 2:4], par[:, LAM:LAM + 1], None, ALU.mult)
                    dve.drain()
                    for t in range(NT):
                        s = slice(t * SEQ, (t + 1) * SEQ)
                        last = V.scalar_tensor_tensor(out=probs[:, 1, s], in0=probs[:, 1, s], scalar=rinv[:, 2 + t:3 + t],
                                                      in1=probs[:, 0, s], op0=ALU.mult, op1=ALU.add)
                else:
                    last = V.tensor_scalar(probs[:, b, :], probs[:, b, :], rinv[:, 2 * b:2 * b + 1], None, ALU.mult)
                last.then_inc(probs_ready, 1)

            def empty_o(l, g):
                if g < 4:
                    dve.wait_ge(o_hi, l * 7 + (g + 1))
                    V.tensor_tensor(mla_oT[:, g, 1, :], O_BANK[:, 0:SEQ], mla_oT[:, g, 0, :].bitcast(F32), ALU.subtract).then_inc(o_emptied, 1)
                elif g < 8:
                    dve.wait_ge(o_full, l * 14 + (g + 1))
                    h = g - 4
                    V.tensor_copy(diff_o[:, :, h * P:(h + 1) * P], O_BANK[:, 0:SEQ].rearrange("p (t d) -> p t d", t=2)).then_inc(o_emptied, 1)
                elif g % 2 == 1:
                    pair = (g - 8) // 2
                    dve.wait_ge(o_hi, l * 7 + (5 + pair))
                    V.tensor_tensor(dil_oT[:, pair, 1, :], O_BANK[:, 0:SEQ], dil_oT[:, pair, 0, :].bitcast(F32), ALU.subtract).then_inc(o_emptied, 1)
                if 4 <= g < 8:
                    h = g - 4
                    dve.drain()
                    cols = diff_o[:, :, h * P:(h + 1) * P]
                    squares_of = head_squares[:].rearrange("p (t d) -> p t d", t=NT)
                    V.tensor_tensor(squares_of, cols, cols, ALU.mult)
                    dve.drain()
                    V.tensor_reduce(ss[:, h:8:4], squares_of, AX.X, ALU.add)
                if g == 7:
                    dve.drain()
                    V.tensor_scalar(mean_eps[:, 0:8], ss[:, 0:8], 1.0 / P, EPS, ALU.mult, ALU.add).then_inc(head_means, 1)

            def normalise_heads(l):
                dve.wait_ge(head_roots, l + 1)
                for t in range(NT):
                    rows = diff_o[:, t, :].rearrange("p (h d) -> p h d", h=4)
                    V.tensor_tensor(rows, rows, inverse_roots[:, 4 * t:4 * t + 4].rearrange("p (h o) -> p h o", o=1).broadcast_to([P, 4, P]),
                                    ALU.mult).then_inc(diff_rows, 1)

            def pre_attn(l):
                dve.wait_ge(squares, l + 1)
                V.tensor_scalar(mean_eps[:, 0:2], ss[:, 0:4:2], EPS, None, ALU.add).then_inc(attn_means, 1)

            def mean(key, first):
                V.tensor_scalar(mean_squares[:, ROOT[key]:ROOT[key] + 1], ss[:, first:first + 1], ss[:, first + 1:first + 2], EPS,
                                ALU.add, ALU.add).then_inc(means_ready, 1)

            def post_gained(l, which, t, h):
                m = post_tile(which, t, h)
                s = slice(h * 512, h * 512 + 512)
                dve.wait_ge(post_squares, l * 8 + (which * 4 + (2 * t if which else t + h) + h + 1))
                V.tensor_tensor(post_scratch(which, t)[:, s], bank[m % NB][:], post_gain[:, s], ALU.mult).then_inc(tile_emptied_dve, 1)

            def post_scratch(which, t):
                return square_ffn[:] if which else merged[:, t, :]

            def post_add(l, which, t):
                j = ROOT[which, t]
                dve.drain()
                dve.wait_ge(roots_ready, l * 6 + (j + 1))
                for h in range(2):
                    s = slice(h * 512, h * 512 + 512)
                    V.scalar_tensor_tensor(out=x[:, t, s], in0=post_scratch(which, t)[:, s], scalar=roots[:, j:j + 1], in1=x[:, t, s],
                                           op0=ALU.mult, op1=ALU.add).then_inc(x_ready, 1)

            def empty_branch(l, n):
                kind = PIECES[n][0]
                f = first_of(n)
                for m in range(f, f + 4):
                    h, t = TILES[m][2:4]
                    s = slice(h * 512, h * 512 + 512)
                    g0 = {"bmla": 0, "bdil": D, "bdiff": 2 * D}[kind] + h * 512
                    wait_tile(dve, l, m)
                    if kind == "bmla":
                        V.scalar_tensor_tensor(out=merged[:, t, s], in0=gates[:, t, g0:g0 + 512], scalar=1.0, in1=bank[m % NB][:],
                                               op0=ALU.add, op1=ALU.mult).then_inc(tile_emptied_dve, 1)
                    else:
                        gs = gates[:, t, g0:g0 + 512]
                        V.scalar_tensor_tensor(out=gs, in0=gs, scalar=1.0, in1=bank[m % NB][:],
                                               op0=ALU.add, op1=ALU.mult).then_inc(tile_emptied_dve, 1)
                        dve.drain()
                        last = V.tensor_tensor(merged[:, t, s], merged[:, t, s], gs, ALU.add)
                        if kind == "bdil":
                            last.then_inc(merged_ready, 1)

            with dve.Fori(0, DEPTH) as l:
                dve.drain()
                V.tensor_copy(par[:], par_all[:, l, :]).then_inc(par_ready, 1)
                dve.drain()
                split_lo(l, 0)
                for step in STEPS:
                    what = step[0]
                    if what == "pre":
                        split_lo(l, 1)
                        pre_attn(l)
                    elif what == "turn":
                        empty_turn(l, step[1])
                        if step[1] == "ffn":
                            split_lo(l, UP0 + 1)
                        if step[1] == "merged":
                            split_lo(l, OUT0 + 1)
                    elif what == "mid":
                        for t in range(NT):
                            dve.wait_ge(post_squares, l * 8 + (t + 3))
                            mean((0, t), 4 + 2 * t)
                            post_gained(l, 0, t, 1)
                            post_add(l, 0, t)
                            dve.wait_ge(ffn_squares, l * NT + (t + 1))
                            mean(("pre", t), 2 * t)
                    elif what == "end":
                        for t in range(NT):
                            dve.drain()
                            if t == 0:
                                dve.wait_ge(gain_landed, (l * 2 + 2) * 16)
                            post_gained(l, 1, t, 0)
                            dve.wait_ge(post_squares, l * 8 + (4 + 2 * t + 2))
                            mean((1, t), 4 + 2 * t)
                            post_gained(l, 1, t, 1)
                            post_add(l, 1, t)
                    elif what == "latent":
                        dve.wait_ge(lat_squares, l * 2 + 2)
                        V.tensor_scalar(mean_eps[:, 0:4:2], ss[:, 0:4:2], 1.0 / Q_RANK, EPS, ALU.mult, ALU.add)
                        V.tensor_scalar(mean_eps[:, 1:4:2], ss[:, 1:4:2], 1.0 / KV_RANK, EPS, ALU.mult, ALU.add)
                        dve.drain().then_inc(latent_means, 1)
                        dve.wait_ge(latent_roots, l + 1)
                        for t in range(NT):
                            for j, (c0, n) in enumerate(((0, Q_RANK), (Q_RANK, KV_RANK))):
                                last = V.tensor_scalar(mla_seq[:, t, c0:c0 + n], mla_seq[:, t, c0:c0 + n], inverse_roots[:, 2 * t + j:2 * t + j + 1], None, ALU.mult)
                        last.then_inc(lat_normed, 1)
                    elif what == "score":
                        negmax_of(l, step[1])
                        normalise(l, step[1])
                    elif what == "pv":
                        empty_o(l, step[1])
                    elif what == "heads":
                        normalise_heads(l)
                    elif what == "td":
                        t = step[1]
                        dve.wait_ge(diff_hi, l * 2 + (t + 1))
                        V.tensor_tensor(diff_oT[:, 1, :, t * P:t * P + P], diff_o[:, t, :].rearrange("p (h q) -> p h q", h=4),
                                        diff_oT[:, 0, :, t * P:t * P + P].bitcast(F32), ALU.subtract).then_inc(diff_lo, 1)
                    elif what == "w":
                        n = step[1]
                        kind, c, k0, nk, cols = PIECES[n]
                        if n + 2 < NPIECE and n not in (OUT0 - 1, UP0 - 1):
                            split_lo(l, n + 2)
                        if kind in ("bmla", "bdiff", "bdil") and k0 + nk == K_TOTAL[kind]:
                            empty_branch(l, n)
                        elif kind == "out" and c == 0 and k0 == 4:
                            dve.wait_ge(gain_landed, (l * 2 + 1) * 16)
                            for t in range(NT):
                                post_gained(l, 0, t, 0)
                        elif kind == "up":
                            u, b = c // 2, c % 2
                            dve.wait_ge(conv_mid, l * 2 * NU + (c + 1))
                            for j in range(2):
                                ch = 22 * b + 2 * u + j
                                o = j * SEQ
                                cv, src = conv[:, u % 2, b, :], bank[4 + c % 4]
                                V.scalar_tensor_tensor(out=cv[:, o + 1:o + SEQ], in0=src[:, o:o + SEQ - 1], scalar=par[:, ch:ch + 1],
                                                       in1=cv[:, o + 1:o + SEQ], op0=ALU.mult, op1=ALU.add)
                            dve.drain()
                            for j in range(2):
                                ch = 22 * b + 2 * u + j
                                o = j * SEQ
                                last = V.scalar_tensor_tensor(out=cv[:, o:o + SEQ - 1], in0=src[:, o + 1:o + SEQ], scalar=par[:, 88 + ch:89 + ch],
                                                              in1=cv[:, o:o + SEQ - 1], op0=ALU.mult, op1=ALU.add)
                            last.then_inc(conv_done, 1)
                            if c % 2 == 1:
                                dve.drain()
                                dve.wait_ge(gelu_done, l * NU + (u + 1))
                                V.tensor_tensor(conv[:, u % 2, 1, :], conv[:, u % 2, 1, :], conv[:, u % 2, 0, :], ALU.mult).then_inc(g_ready, 1)
                                dve.wait_ge(g_hi_done, l * NU + (u + 1))
                                V.tensor_tensor(by_class2(g_lo[:, u % 2, :]), own_order2(conv[:, u % 2, 1, :]),
                                                by_class2(g_hi[:, u % 2, :].bitcast(F32)), ALU.subtract).then_inc(g_lo_done, 1)

        @block.tensor
        def _(pe):
            PE = nc.tensor
            pe.sem_inc(piece_used, RING)
            pe.wait_ge(ident_ready, 1)
            def keep_clock(steps, into):
                for _ in range(steps):
                    PE.transpose(into, ident[:], ident[:])

            keep_clock(WARM_UP // 2, bank[7][:, 0:P])
            pe.wait_ge(parameters_landed, 16 * N_PARAMETERS)
            for j in range(3 * DEPTH):
                PE.transpose(bank[0][:, 44 * j:44 * j + 44], par_rows[:, j, :], ident[0:44, 0:44])
            for l in range(DEPTH):
                c0 = 132 * DEPTH + 22 * l
                last = PE.transpose(bank[0][:, c0:c0 + 22], par_rows[0:22, 3 * DEPTH + l, :], ident[0:22, 0:22])
            last.then_inc(par_turned, 1)
            keep_clock(WARM_UP // 2, bank[7][:, 0:P])

            def passes(dst, lhs, rhs_hi, rhs_lo, start, stop):
                PE.matmul(dst, lhs[1], rhs_hi, start=start, stop=False)
                PE.matmul(dst, lhs[0], rhs_lo, start=False, stop=False)
                return PE.matmul(dst, lhs[0], rhs_hi, start=False, stop=stop)

            def rows(hi, lo, k, t):
                return hi[:, k, t * P:(t + 1) * P], lo[:, k, t * P:(t + 1) * P]

            def lhs_of(kind, c, k, t):
                if kind in ("mla", "diff", "dil", "gate", "out"):
                    return rows(hT_hi, hT_lo, k, t)
                if kind == "uq":
                    return rows(latT_hi, latT_lo, k, t)
                if kind == "ukv":
                    return rows(latT_hi, latT_lo, 3 + k, t)
                if kind == "bmla":
                    return mla_oT[:, k, 0, t * P:(t + 1) * P], mla_oT[:, k, 1, t * P:(t + 1) * P]
                if kind == "bdiff":
                    return diff_oT[:, 0, k, t * P:(t + 1) * P], diff_oT[:, 1, k, t * P:(t + 1) * P]
                if kind == "bdil":
                    return dil_oT[:, k, 0, t * P:(t + 1) * P], dil_oT[:, k, 1, t * P:(t + 1) * P]
                u = c
                return g_hi[:, u % 2, k * SEQ + t * P:k * SEQ + t * P + P], g_lo[:, u % 2, k * SEQ + t * P:k * SEQ + t * P + P]

            def wait_turned(l, kind, c, k):
                what = {"mla": "attn", "uq": "latent", "ukv": "latent", "out": "merged", "up": "ffn"}.get(kind)
                if what is None or c != 0:
                    return
                kk = k + 3 if kind == "ukv" else k
                pe.wait_ge(turn_emptied, l * NTURN + (TURN_BEFORE[what] + kk // 2 + 1))

            def use_piece(l, n):
                kind, c, k0, nk, cols = PIECES[n]
                if n in JOINED:
                    return
                parts = [n - 1, n] if n - 1 in JOINED else [n]
                hi, lo = cut(w_hi, n), cut(w_lo, n)
                pe.wait_ge(lo_done, l * NPIECE + (n + 1 + RING))
                if kind == "up":
                    u, b = c // 2, c % 2
                    if c >= 4:
                        pe.wait_ge(conv_done, BASE + l * 2 * NU + (c - 3))
                    for j in range(2):
                        for k in range(8):
                            if j == 0:
                                wait_turned(l, kind, c, k)
                            last = passes(bank[4 + c % 4][:, j * SEQ:(j + 1) * SEQ],
                                          (hi[:, k, j * P:(j + 1) * P], lo[:, k, j * P:(j + 1) * P]),
                                          hT_hi[:, k, :], hT_lo[:, k, :], k == 0, k == 7)
                    last.then_inc(piece_used, 1)
                    return
                halves = 2 if cols == 1024 else 1
                width = cols // halves
                if kind == "down":
                    f = NTILE - 4
                    pe.wait_ge(g_lo_done, l * NU + (c + 1))
                    start, stop = c == 0, c == NU - 1
                else:
                    f = first_of(n)
                    start, stop = PIECES[parts[0]][2] == 0, k0 + nk == K_TOTAL[kind]
                if kind == "bmla" or kind == "bdil":
                    pe.wait_ge(o_emptied, BASE + l * 11 + (4 if kind == "bmla" else 11))
                if kind == "bdiff":
                    pe.wait_ge(diff_lo, l * 2 + 2)
                for m in range(f, f + NT * halves):
                    h, t = TILES[m][2:4]
                    if start:
                        if m >= NB:
                            who, count = emptied(m - NB)
                            if who == "act":
                                pe.wait_ge(tile_emptied_act, l * N_ACT + count)
                            else:
                                pe.wait_ge(tile_emptied_dve, BASE + l * N_DVE + count)
                        else:
                            pe.wait_ge(tile_emptied_dve, BASE + l * N_DVE + 0)
                    for part in parts:
                        hi, lo = cut(w_hi, part), cut(w_lo, part)
                        p_k0, p_nk = PIECES[part][2:4]
                        for k in range(p_nk):
                            kk = k if kind == "down" else p_k0 + k
                            if m == f:
                                wait_turned(l, kind, c, kk)
                            last = passes(bank[m % NB][:, 0:width], lhs_of(kind, c, kk, t),
                                          hi[:, k, h * 512:h * 512 + width], lo[:, k, h * 512:h * 512 + width],
                                          start and k == 0 and part == parts[0], stop and k == p_nk - 1 and part == n)
                        if m == f + NT * halves - 1:
                            last.then_inc(piece_used, 1)
                    if stop and m not in GROUP_END:
                        last.then_inc(tile_full, 1)

            def turn(l, what):
                before = TURN_BEFORE[what]
                if what == "attn":
                    pe.wait_ge(conv_done, BASE + l * 2 * NU)
                else:
                    pe.wait_ge(turn_emptied, l * NTURN + before)
                if what == "latent":
                    pe.wait_ge(lat_normed, l + 1)
                if what == "merged":
                    pe.wait_ge(o_emptied, BASE + l * 11 + 11)
                    pe.wait_ge(t_emptied, BASE + l * NTB + NTB)
                banks = TURN_BANKS[what]
                if what == "merged":
                    order = [(b, t) for b in range(len(banks)) for t in range(NT)]
                else:
                    order = [(b, t) for t in range(NT) for b in range(len(banks))]
                for b, t in order:
                    k0, nk = banks[b]
                    h = b // 2
                    if b == 0 and what in WAITS:
                        keep_clock(WAITS[what][t], bank[7][:, 3 * P:4 * P])
                    if b % 2 == 0:
                        if what == "attn":
                            pe.wait_ge(x_landed, 16 * 2)
                            pe.wait_ge(x_ready, l * 8 + (2 * t + h + 1))
                        elif what == "ffn":
                            pe.wait_ge(xn_done, l * 4 + (2 * t + h + 1))
                        elif what == "merged":
                            pe.wait_ge(merged_ready, l * 4 + (2 * h + t + 1))
                    rows = {"latent": mla_seq, "merged": merged, "attn": x, "ffn": xn}[what]
                    for k in range(nk):
                        last = PE.transpose(bank[4 + b][:, k * SEQ + t * P:k * SEQ + t * P + P],
                                            rows[:, t, (k0 + k) * P:(k0 + k + 1) * P], ident[:])
                    if t == NT - 1:
                        last.then_inc(turn_full, 1)
                if what in WAITS:
                    keep_clock(WAITS[what][NT], bank[3][:, 0:P])

            def wait_t(l, key):
                n = T_OF[key]
                pe.wait_ge(t_emptied, BASE + l * NTB + (max(n - 1, 0) if n < N_EARLY else n))
                if key == ("tq", 0):
                    pe.wait_ge(turn_emptied, l * NTURN + 7)
                return t_bank(n)

            def wait_heads(l, i):
                if i < 8:
                    need = [("uq", i // 4), ("ukv", i // 4)]
                elif i < 16:
                    need = [("diff", 0), ("diff", 1)]
                else:
                    need = [("dil", c) for c in range(9) if c % 3 < 2]
                last = max(T_OF["tq", s] for s, n in enumerate(STAGED) if TILES[n][0:2] in need)
                pe.wait_ge(t_emptied, BASE + l * NTB + (last + 1))

            def scores(l, i):
                if i in (0, 4, 8, 16):
                    wait_heads(l, i)
                b = S_BANK[i % 2]
                qt = i % 2
                q = slice(qt * P, qt * P + P)
                if i >= 2:
                    pe.wait_ge(exp_done, l * 28 + (i - 1))
                if i < 8:
                    pair = i // 2
                    for h in range(2):
                        last = PE.matmul(b[:, h * SEQ:(h + 1) * SEQ], mla_qT[0:QK_M, 2 * pair + h, q], mla_kT[0:QK_M, 2 * pair + h, :], start=True, stop=True)
                elif i < 16:
                    head, m = i // 2 - 4, i % 2
                    r = slice(64 * m, 64 * m + 64)
                    for t in range(NT):
                        last = PE.matmul(b[:, t * SEQ:(t + 1) * SEQ], diff_qT[r, head, t * P:(t + 1) * P], diff_kT[r, head, :], start=True, stop=True)
                else:
                    head = i // 2 - 8
                    pe.wait_ge(masks_ready, 1)
                    r = slice(64 * (head % 2), 64 * (head % 2) + 64)
                    PE.matmul(b[:], ident_b[:], mask[:, qt, :], start=True, stop=False, skip_group_check=True)
                    PE.matmul(b[:, 0:SEQ], dil_qT[r, head // 2, 0, q], dil_kT[r, head // 2, 0, :], start=False, stop=True, skip_group_check=True)
                    for g in (1, 2):
                        last = PE.matmul(b[:, P + g * P:2 * P + g * P], dil_qT[r, head // 2, g, q], dil_kT[r, head // 2, g, q],
                                         start=False, stop=True, skip_group_check=True)
                last.then_inc(score_full, 1)

            def products(l, g):
                pt = probsT[:, g % 2, :, :]
                pe.wait_ge(t_emptied, BASE + l * NTB + (T_OF[("tp", 2 * g + 1)] + 1))
                done = g if g <= 8 else 8 + (g - 8) // 2
                if g == 0:
                    pe.wait_ge(turn_emptied, l * NTURN + 7)
                pe.wait_ge(o_emptied, BASE + l * 11 + done)
                if g < 4:
                    for h in range(2):
                        for kt in range(2):
                            last = PE.matmul(O_BANK[64 * h:64 * h + 64, 0:SEQ], v_mla[:, kt, 2 * g + h, :], pt[:, 2 * h + kt, :],
                                             start=kt == 0, stop=kt == 1)
                elif g < 8:
                    h = g - 4
                    for t in range(NT):
                        for kt in range(2):
                            last = PE.matmul(O_BANK[:, t * P:t * P + P], pt[:, kt, t * P:t * P + P], v_diff[:, kt, h * P:(h + 1) * P],
                                             start=kt == 0, stop=kt == 1)
                else:
                    head = g - 8
                    o = 64 * (head % 2)
                    vs = slice(head * HD, head * HD + HD)
                    for kt in range(2):
                        PE.matmul(O_BANK[o:o + 64, 0:SEQ], v_dil[:, kt, 0, vs], pt[:, kt, :], start=kt == 0, stop=False, skip_group_check=True)
                    for dg in (1, 2):
                        for t in range(NT):
                            last = PE.matmul(O_BANK[o:o + 64, t * P:t * P + P], v_dil[:, t, dg, vs], pt[:, 1 + dg, t * P:t * P + P],
                                             start=False, stop=dg == 2, skip_group_check=True)
                last.then_inc(o_full, 1)

            with pe.Fori(0, DEPTH) as l:
                for step in STEPS:
                    what = step[0]
                    if what == "turn":
                        turn(l, step[1])
                    elif what == "w":
                        use_piece(l, step[1])
                    elif what == "score":
                        scores(l, step[1])
                    elif what == "pv":
                        products(l, step[1])
                    elif what == "tq":
                        s = step[1]
                        T_BANK = wait_t(l, step)
                        pe.wait_ge(roped, l * NSTAGE + (s + 1))
                        kind = TILES[STAGED[s]][0]
                        st = stage[:, s % SRING, :]
                        if kind in ("uq", "ukv"):
                            for h in range(4):
                                last = PE.transpose(T_BANK[0:QK_M, h * P:(h + 1) * P], st[:, h * QK_M:(h + 1) * QK_M], ident[:])
                        else:
                            for h in range(4 if kind == "diff" else 3):
                                last = PE.transpose(T_BANK[:, h * P:(h + 1) * P], st[:, h * P:(h + 1) * P], ident[:])
                        last.then_inc(t_full, 1)
                    elif what == "tp":
                        i = step[1]
                        T_BANK = wait_t(l, step)
                        pe.wait_ge(probs_ready, l * 28 + (i + 1))
                        for b in range(4):
                            last = PE.transpose(T_BANK[:, b * P:(b + 1) * P], probs[:, i % 2, b * P:(b + 1) * P], ident[:])
                        last.then_inc(t_full, 1)
                    elif what == "td":
                        t = step[1]
                        T_BANK = wait_t(l, step)
                        pe.wait_ge(diff_rows, l * 2 + (t + 1))
                        for h in range(4):
                            last = PE.transpose(T_BANK[:, h * P:(h + 1) * P], diff_o[:, t, h * P:(h + 1) * P], ident[:])
                        last.then_inc(t_full, 1)


ROOT = {key: j for j, key in enumerate(((0, 0), ("pre", 0), (0, 1), ("pre", 1), (1, 0), (1, 1)))}


def post_tile(which, t, h):
    return NTILE - 4 + 2 * t + h if which else NTILE - 8 + 2 * h + t


def first_of(n):
    kind, c = PIECES[n][0:2]
    while n not in FIRST_TILE or PIECES[n][0:2] != (kind, c):
        n -= 1
    return FIRST_TILE[n]


def tiles_of(n):
    return 4 if PIECES[n][4] == 1024 else 2


_INS = ['x', 'positions', 'attn_pre_norm', 'w_in', 'mla_q_norm', 'mla_w_uq', 'mla_kv_norm', 'mla_w_ukv', 'diff_lambda',
        'diff_subln', 'w_branch_mla', 'w_branch_dil', 'w_branch_diff', 'w_out', 'attn_post_norm', 'ffn_pre_norm', 'w_up',
        'ffn_conv', 'w_down', 'ffn_post_norm']


def kernel(**inputs):
    import concourse.bacc as _bacc
    from concourse.bass_utils import run_bass_kernel_spmd as _run

    nc = _bacc.Bacc("TRN2", target_bir_lowering=False, num_devices=1)
    arrays, args = {}, {}
    for name in _INS:
        v = np.ascontiguousarray(inputs[name])
        arrays[f"in_{name}_dram"] = v
        args[name] = nc.dram_tensor(f"in_{name}_dram", v.shape, mybir.dt.from_np(v.dtype), kind="ExternalInput").ap()
    out = nc.dram_tensor("out_dram", (1, SEQ, D), F32, kind="ExternalOutput").ap()
    build_trunk(nc, args, out)
    r = _run(nc, [arrays], core_ids=[0])
    return r.results[0]["out_dram"]
```
